# Optimizing a Trainium2 kernel written in Bass

```python
import math
import jax, jax.numpy as jnp
from jax import lax
import numpy as np

D_MODEL = 1024
BATCH = 1
SEQ = 128
DEPTH = 1
DEC_BATCH = 1
DEC_SEQ = 1024
PAST_LEN = 256

GRID_W = 64
D_MIX = D_MODEL
POOL_W = D_MIX // 2
POOL_WINDOWS = (2, 4, 8, 16)
N_POOL_GROUPS = 4
POOL_GROUP_DIM = POOL_W // N_POOL_GROUPS
MLSTM_W = D_MIX - POOL_W
MLSTM_HEADS = 4
MLSTM_HEAD_DIM = MLSTM_W // MLSTM_HEADS
QK_CONV_W = 3
CHUNK = 64
D_FF = 2816
N_GATE_COLS = 4 * MLSTM_HEADS
IN_COLS = POOL_W + 4 * MLSTM_W + N_GATE_COLS
ALPHA = (2.0 * DEPTH) ** 0.25
BETA = (8.0 * DEPTH) ** -0.25
LN_EPS = 1e-5

kernel_name = 'hybrid_pool_mlstm_diffusion_step'

def layer_norm(x, g=None, b=None):
    xf = x.astype(jnp.float32)
    mu = xf.mean(-1, keepdims=True)
    var = jnp.square(xf - mu).mean(-1, keepdims=True)
    y = (xf - mu) * lax.rsqrt(var + LN_EPS)
    if g is not None:
        y = y * g + b
    return y.astype(x.dtype)

def modulate(x, shift, scale):
    return x * (1.0 + scale[:, None, :]) + shift[:, None, :]

def window_mean(x, w, axis):
    L = x.shape[axis]
    cs = jnp.cumsum(x.astype(jnp.float32), axis=axis)
    zero = jnp.zeros_like(lax.slice_in_dim(cs, 0, 1, axis=axis))
    S = jnp.concatenate([zero, cs], axis=axis)
    t = jnp.arange(L)
    hi = jnp.minimum(t + w // 2, L)
    lo = jnp.maximum(t - w // 2, 0)
    s = jnp.take(S, hi, axis=axis) - jnp.take(S, lo, axis=axis)
    shape = [1] * x.ndim
    shape[axis] = L
    return s / (hi - lo).astype(jnp.float32).reshape(shape)

def pool_mixer(xp, w_pool, pool_scale):
    B, R, W, _ = xp.shape
    grp = xp.reshape(B, R, W, N_POOL_GROUPS, POOL_GROUP_DIM)
    outs = []
    for gi, win in enumerate(POOL_WINDOWS):
        xg = grp[..., gi, :]
        outs.append(window_mean(window_mean(xg, win, 1), win, 2) - xg)
    y = jnp.stack(outs, axis=-2)
    y = jnp.einsum('brwgc,gcd->brwgd', y, w_pool)
    return y.reshape(B, R * W, POOL_W) * pool_scale

def dwconv1d_centred(x, w):
    L = x.shape[1]
    xp = jnp.pad(x, ((0, 0), (1, 1), (0, 0)))
    return xp[:, :L] * w[0] + xp[:, 1:L + 1] * w[1] + xp[:, 2:] * w[2]

def mlstm_chunkwise(q, k, v, i_pre, f_pre, C0, n0, m0):
    B, H, L, DH = q.shape
    nc = L // CHUNK
    f32 = jnp.float32

    def chunks(a):
        a = a.astype(f32).reshape((B, H, nc, CHUNK) + a.shape[3:])
        return jnp.moveaxis(a, 2, 0)

    xs = (chunks(q), chunks(k), chunks(v), chunks(i_pre), chunks(jax.nn.log_sigmoid(f_pre.astype(f32))))
    tri = jnp.tril(jnp.ones((CHUNK, CHUNK), dtype=bool))

    def step(carry, inp):
        C, n, m = carry
        qb, kb, vb, li, lf = inp
        b = jnp.cumsum(lf, axis=-1)
        log_d = jnp.where(tri, b[..., :, None] - b[..., None, :] + li[..., None, :], -jnp.inf)
        inter = b + m[..., None]
        m_t = jnp.maximum(inter, log_d.max(-1))
        d = jnp.exp(log_d - m_t[..., None])
        a_inter = jnp.exp(inter - m_t)
        s = jnp.einsum('bhtd,bhsd->bhts', qb, kb) * d
        num = a_inter[..., None] * jnp.einsum('bhtd,bhde->bhte', qb, C) + jnp.einsum('bhts,bhse->bhte', s, vb)
        den = a_inter * jnp.einsum('bhtd,bhd->bht', qb, n) + s.sum(-1)
        h = num / jnp.maximum(jnp.abs(den), jnp.exp(-m_t))[..., None]
        g = b[..., -1]
        log_w = g[..., None] - b + li
        m_new = jnp.maximum(g + m, log_w.max(-1))
        w = jnp.exp(log_w - m_new[..., None])
        decay = jnp.exp(g + m - m_new)
        C_new = decay[..., None, None] * C + jnp.einsum('bhs,bhsd,bhse->bhde', w, kb, vb)
        n_new = decay[..., None] * n + jnp.einsum('bhs,bhsd->bhd', w, kb)
        return (C_new, n_new, m_new), h

    (C, n, m), hs = lax.scan(step, (C0.astype(f32), n0.astype(f32), m0.astype(f32)), xs)
    h = jnp.moveaxis(hs, 0, 2).reshape(B, H, L, DH)
    return h, (C, n, m)

def mlstm_mixer(q, k, v, o, gates, w_qk_conv, b_gates, hn_g, st0):
    B, L, _ = q.shape
    qk = jax.nn.silu(dwconv1d_centred(jnp.concatenate([q, k], axis=-1), w_qk_conv))
    q, k = jnp.split(qk, 2, axis=-1)

    def heads(a):
        return a.reshape(B, L, MLSTM_HEADS, MLSTM_HEAD_DIM).transpose(0, 2, 1, 3)

    qh, kh, vh = heads(q), heads(k) * (MLSTM_HEAD_DIM ** -0.5), heads(v)
    g = (gates + b_gates).reshape(B, L, 4, MLSTM_HEADS).transpose(2, 0, 3, 1)
    C0, n0, m0 = st0
    h_f, (Cf, nf, mf) = mlstm_chunkwise(qh, kh, vh, g[0], g[1], C0[:, 0], n0[:, 0], m0[:, 0])
    flip = lambda a: jnp.flip(a, axis=2)
    h_b, (Cb, nb, mb) = mlstm_chunkwise(flip(qh), flip(kh), flip(vh), jnp.flip(g[2], -1), jnp.flip(g[3], -1),
                                        C0[:, 1], n0[:, 1], m0[:, 1])
    h = h_f + flip(h_b)
    mu = h.mean(-1, keepdims=True)
    var = jnp.square(h - mu).mean(-1, keepdims=True)
    h = ((h - mu) * lax.rsqrt(var + LN_EPS)).transpose(0, 2, 1, 3).reshape(B, L, MLSTM_W) * hn_g
    out = (jax.nn.sigmoid(o) * h).astype(q.dtype)
    dt = q.dtype
    new_state = (jnp.stack([Cf, Cb], axis=1).astype(dt), jnp.stack([nf, nb], axis=1).astype(dt),
                 jnp.stack([mf, mb], axis=1).astype(dt))
    return out, new_state

def conv_ffn(h, rows, cols, w_up, w_dw, b_dw, w_down):
    B, L, _ = h.shape
    up = h @ w_up
    a, g = jnp.split(up, 2, axis=-1)
    g4 = g.reshape(B, rows, cols, D_FF)
    g4 = lax.conv_general_dilated(g4, w_dw.reshape(3, 3, 1, D_FF).astype(g4.dtype), (1, 1), 'SAME',
                                  dimension_numbers=('NHWC', 'HWIO', 'NHWC'), feature_group_count=D_FF)
    g = g4.reshape(B, L, D_FF) + b_dw
    return (jax.nn.gelu(g) * a) @ w_down

def trunk_layer(x, cond, rows, cols, st0, p):
    B, L, _ = x.shape
    ada = jax.nn.silu(cond) @ p['w_ada'] + p['b_ada']
    sh1, sc1, g1, sh2, sc2, g2 = jnp.split(ada, 6, axis=-1)
    h = modulate(layer_norm(x), sh1, sc1)
    proj = h @ p['w_in']
    o1 = POOL_W
    xp = proj[..., :o1]
    q = proj[..., o1:o1 + MLSTM_W]
    k = proj[..., o1 + MLSTM_W:o1 + 2 * MLSTM_W]
    v = proj[..., o1 + 2 * MLSTM_W:o1 + 3 * MLSTM_W]
    o = proj[..., o1 + 3 * MLSTM_W:o1 + 4 * MLSTM_W]
    gates = proj[..., o1 + 4 * MLSTM_W:]
    pool_out = pool_mixer(xp.reshape(B, rows, cols, POOL_W), p['w_pool'], p['pool_scale']).astype(x.dtype)
    ml_out, st_new = mlstm_mixer(q, k, v, o, gates, p['w_qk_conv'], p['b_gates'], p['hn_g'], st0)
    mix = jnp.concatenate([pool_out, ml_out], axis=-1) @ p['w_out']
    x = layer_norm(ALPHA * x + g1[:, None, :] * mix, p['ln1_g'], p['ln1_b'])
    h = modulate(layer_norm(x), sh2, sc2)
    ffn = conv_ffn(h, rows, cols, p['w_up'], p['w_dw'], p['b_dw'], p['w_down'])
    x = layer_norm(ALPHA * x + g2[:, None, :] * ffn, p['ln2_g'], p['ln2_b'])
    return x, st_new

def setup_inputs(seed: int = 0) -> dict:
    key = jax.random.key(seed)
    ks = jax.random.split(key, 26)
    f32 = jnp.float32

    def nrm(k, shape, s):
        return jax.random.normal(k, shape, f32) * s

    H, DH = MLSTM_HEADS, MLSTM_HEAD_DIM
    gate_base = jnp.array([0.0, 3.0, 0.0, 3.0], f32)[None, :, None]
    return {
        'x_prompt': nrm(ks[0], (BATCH, SEQ, D_MODEL), 1.0),
        'x_sample': nrm(ks[1], (DEC_BATCH, DEC_SEQ, D_MODEL), 1.0),
        'c': nrm(ks[2], (DEC_BATCH, D_MODEL), 1.0),
        'state_C': nrm(ks[3], (DEC_BATCH, DEPTH, 2, H, DH, DH), DH ** -0.5),
        'state_n': nrm(ks[4], (DEC_BATCH, DEPTH, 2, H, DH), 0.5),
        'state_m': nrm(ks[5], (DEC_BATCH, DEPTH, 2, H), 1.0),
        'c_ctx': nrm(ks[6], (D_MODEL,), 1.0),
        'w_ada': nrm(ks[7], (DEPTH, D_MODEL, 6 * D_MODEL), D_MODEL ** -0.5),
        'b_ada': nrm(ks[8], (DEPTH, 6 * D_MODEL), 0.02),
        'w_in': nrm(ks[9], (DEPTH, D_MODEL, IN_COLS), D_MODEL ** -0.5),
        'b_gates': (gate_base + nrm(ks[10], (DEPTH, 4, H), 0.5)).reshape(DEPTH, N_GATE_COLS),
        'w_qk_conv': nrm(ks[11], (DEPTH, QK_CONV_W, 2 * MLSTM_W), QK_CONV_W ** -0.5),
        'hn_g': 1.0 + nrm(ks[12], (DEPTH, MLSTM_W), 0.05),
        'w_pool': nrm(ks[13], (DEPTH, N_POOL_GROUPS, POOL_GROUP_DIM, POOL_GROUP_DIM), POOL_GROUP_DIM ** -0.5),
        'pool_scale': 1.0 + nrm(ks[14], (DEPTH, POOL_W), 0.05),
        'w_out': nrm(ks[15], (DEPTH, D_MIX, D_MODEL), BETA * D_MIX ** -0.5),
        'ln1_g': 1.0 + nrm(ks[16], (DEPTH, D_MODEL), 0.05),
        'ln1_b': nrm(ks[17], (DEPTH, D_MODEL), 0.02),
        'w_up': nrm(ks[18], (DEPTH, D_MODEL, 2 * D_FF), D_MODEL ** -0.5),
        'w_dw': nrm(ks[19], (DEPTH, 3, 3, D_FF), 1.0 / 3.0),
        'b_dw': nrm(ks[20], (DEPTH, D_FF), 0.02),
        'w_down': nrm(ks[21], (DEPTH, D_FF, D_MODEL), BETA * D_FF ** -0.5),
        'ln2_g': 1.0 + nrm(ks[22], (DEPTH, D_MODEL), 0.05),
        'ln2_b': nrm(ks[23], (DEPTH, D_MODEL), 0.02),
    }

def reference(x_prompt, x_sample, c, state_C, state_n, state_m, c_ctx, w_ada, b_ada, w_in, b_gates,
              w_qk_conv, hn_g, w_pool, pool_scale, w_out, ln1_g, ln1_b, w_up, w_dw, b_dw, w_down,
              ln2_g, ln2_b):
    B_p, L_p, _ = x_prompt.shape
    L_s = x_sample.shape[1]
    rows = L_s // GRID_W
    dt = x_prompt.dtype
    zero_state = (jnp.zeros((B_p, 2, MLSTM_HEADS, MLSTM_HEAD_DIM, MLSTM_HEAD_DIM), dt),
                  jnp.zeros((B_p, 2, MLSTM_HEADS, MLSTM_HEAD_DIM), dt),
                  jnp.zeros((B_p, 2, MLSTM_HEADS), dt))
    y_p, y_s = x_prompt, x_sample
    Cs, ns, ms = [], [], []
    for l in range(DEPTH):
        p = dict(w_ada=w_ada[l], b_ada=b_ada[l], w_in=w_in[l], b_gates=b_gates[l], w_qk_conv=w_qk_conv[l],
                 hn_g=hn_g[l], w_pool=w_pool[l], pool_scale=pool_scale[l], w_out=w_out[l], ln1_g=ln1_g[l],
                 ln1_b=ln1_b[l], w_up=w_up[l], w_dw=w_dw[l], b_dw=b_dw[l], w_down=w_down[l], ln2_g=ln2_g[l],
                 ln2_b=ln2_b[l])
        y_p, (Cl, nl, ml) = trunk_layer(y_p, c_ctx[None, :], 1, L_p, zero_state, p)
        Cs.append(Cl)
        ns.append(nl)
        ms.append(ml)
        y_s, _ = trunk_layer(y_s, c, rows, GRID_W, (state_C[:, l], state_n[:, l], state_m[:, l]), p)
    new_state_C = jnp.stack(Cs, axis=1)
    new_state_n = jnp.stack(ns, axis=1)
    new_state_m = jnp.stack(ms, axis=1)
    return (y_p, y_s, new_state_C, new_state_n, new_state_m)


_drawn_inputs = setup_inputs


def setup_inputs(seed=0):
    import zlib

    import numpy as np

    out = dict(_drawn_inputs(seed))
    spreads = {}
    factors = {'state_C': 8.0,
     'state_n': 8.0,
     'state_m': 8.0,
     'hn_g': 8.0,
     'pool_scale': 4.685,
     'ln1_b': 2.748,
     'b_dw': 8.0,
     'ln2_b': 2.913}
    for name, (base, spread) in spreads.items():
        noise = np.random.default_rng([zlib.crc32(name.encode()), seed]).standard_normal(out[name].shape)
        drawn = base * np.exp(spread * noise) if base else spread * noise
        out[name] = __import__('jax').numpy.asarray(drawn.astype(out[name].dtype))
    for name, factor in factors.items():
        out[name] = (out[name] * factor).astype(out[name].dtype)
    return out
```

```python
import concourse.bass as bass
from concourse import mybir
import numpy as np
from contextlib import ExitStack

F32 = mybir.dt.float32
F32R = mybir.dt.float32r
ALU = mybir.AluOpType
ACT = mybir.ActivationFunctionType

P = 128
DM = 1024
KT = DM // P
LAT, CTX = 1024, 128
T = LAT + CTX
NT = T // P
LT = NT - 1
GN = 384
NG = T // GN
GT = GN // P
H = 4
GRID_W, GRID_H = 64, 16
WINDOWS = (2, 4, 8, 16)
FF = 2816
FT = FF // P
NGATE = 16
ALPHA = 2.0 ** 0.25
EPS = 1e-5
QK_SCALE = float(P) ** -0.5

UC = 512
RAWN = 4
NPROJ = 16
U_C = 2 * NPROJ
U_OUT = U_C + 2 * H
U_UP = U_OUT + NG * KT * 2
U_DOWN = U_UP + FT * 4
U_END = U_DOWN + NG * FT * 2

V_C, V_CC, V_BADA, V_HN, V_PS, V_CONV, V_BDW, NV = 0, 8, 16, 64, 68, 72, 96, 118
A_SH1, A_SC1, A_G1, A_SH2, A_SC2, A_G2 = (KT * i for i in range(6))
AC = 256
N_ADA1 = 2 * DM // AC
N_ADA = 6 * DM // AC
ADA1_RING = 6
ADA_AT = 2 * 6 * KT
NTAP = 9
DIR = 64
PADW = GRID_W + 16
PADC = CTX + 16


def proj_col(tile):
    kind, j = tile // H, tile % H
    return (0, 3 * H, H, 2 * H, 4 * H)[kind] * P + j * P


JOBS = {1: ("gT",), 4: ("grow",), 6: ("mcol",), 8: ("tok",)}
for _n in range(12):
    JOBS[10 + _n] = ("v", _n // 3, _n % 3)
for _n in range(10):
    JOBS[22 + _n] = ("pool", _n // 3, _n % 3)
LATE_JOBS = (("pool", 3, 1), ("pool", 3, 2))


def layer(nc, x_prompt, x_sample, c, state_C, state_n, state_m, c_ctx, w_ada, b_ada, w_in, b_gates,
          w_qk_conv, hn_g, w_pool, pool_scale, w_out, ln1_g, ln1_b, w_up, w_dw, b_dw, w_down,
          ln2_g, ln2_b, inv_count, y_prompt, y_sample, new_C, new_n, new_m, scan_rows, pool_out, x1_rows):
    with ExitStack() as stack, nc.allow_non_contiguous_dma(reason="normaliser column of the state, stabiliser rows"):
        def sem(name):
            return stack.enter_context(nc.semaphore(name))

        top = [(nc.sbuf_base + 63) // 64 * 64]

        def place(name, shape, at=None, dt=F32):
            size = 4 * int(np.prod(shape[1:]))
            if at is None:
                at = top[0]
                top[0] = (at + size + 31) // 32 * 32
            return nc.alloc_sbuf_tensor_at(name, shape, dt, offset=(at + 31) // 32 * 32)

        raw = place("raw", [P, RAWN, UC])
        whi = place("whi", [P, 2, UC], dt=F32R)
        wlo = place("wlo", [P, 2, UC], dt=F32R)
        ident = place("ident", [P, P])
        colv = place("colv", [P, NV])
        dwc = place("dwc", [P, NTAP * FT])
        adaT = place("adaT", [P, 6 * KT, 2])
        ada1p = place("ada1p", [P, 2, KT, 2])
        neghalf = place("neghalf", [P, H, 1])
        one11 = place("one11", [P, 1])
        stats = place("stats", [P, 4, 12])
        mv = place("mv", [P, 4, 2])
        rstd = place("rstd", [P, 4, 1])
        taps = place("taps", [P, NTAP + 1])
        wgr = place("wgr", [P, KT, NGATE])
        wghi = place("wghi", [P, KT, NGATE], dt=F32R)
        wglo = place("wglo", [P, KT, NGATE], dt=F32R)
        M0 = top[0]
        big = 4 * KT * T

        h1hi = place("h1hi", [P, KT, T], M0, F32R)
        h1lo = place("h1lo", [P, KT, T], M0 + big, F32R)
        qk_at = M0 + 2 * big
        qk = place("qk", [P, 2 * H, T], qk_at)
        v1_at = qk_at + big
        v1 = place("v1", [P, NT, H, P + 1], v1_at)
        hacc_at = (v1_at + 4 * NT * H * (P + 1) + 31) // 32 * 32
        hacc = place("hacc", [P, NT, H, P], hacc_at)
        poolA = place("poolA", [P, 2048], hacc_at)
        poolB = place("poolB", [P, 2048], hacc_at + 8192)
        adaw1 = place("adaw1", [P, ADA1_RING, KT, AC], qk_at)
        xt_at = qk_at + 4 * ADA1_RING * KT * AC
        xt = place("xt", [P, NT, DM], xt_at)
        work_at = hacc_at + 4 * NT * H * P
        work = place("work", [P, 4, T], work_at)
        past_xt = xt_at + 4 * NT * DM
        assert work_at < past_xt
        rowsv = place("rowsv", [P, P], past_xt)
        rowsd = place("rowsd", [P, 2, P], past_xt + 512)
        bgate = place("bgate", [P, NGATE], past_xt + 1536)
        graw = place("graw", [NGATE, T], past_xt + 1600)
        assert past_xt + 1600 + 4 * T <= work_at + 16 * T
        wpl = place("wpl", [P, H, P], work_at + 4 * 2 * T)
        po = place("po", [P, 2, GN], work_at + 4 * 2 * T + 4 * T + 64)
        top[0] = work_at + 16 * T
        cs_at = top[0]
        Cs = place("Cs", [P, 2, H, P + 1])
        tok = place("tok", [P, 3, P])
        decb = place("decb", [P, P])
        gcol = place("gcol", [P, 8])
        grow = place("grow", [1, 2, P])
        mrow = place("mrow", [1, P])
        m0row = place("m0row", [1, 2 * H])
        tmp_at = top[0]
        Dm = place("Dm", [P, 2, 2, H, P])
        Qa = place("Qa", [P, 2, H, P])
        kw = place("kw", [P, 2, H, P])
        mvh = place("mvh", [P, 2, H, 2])
        sth = place("sth", [P, 2, H, 6])
        rsh = place("rsh", [P, 2, H, 1])
        rden = place("rden", [P, 2, 1])
        tmph = place("tmph", [P, 2, P])
        assert top[0] <= nc.sbuf_usable_end, (top[0], nc.sbuf_usable_end)
        top[0] = tmp_at
        hm = place("hm", [P, 2, KT, P], tmp_at)
        adaw = place("adaw", [P, 2, KT // 2, AC])
        arow = place("arow", [2, 2, AC])
        gi, gf, li, fr, lf, Bc, Ac, CM, nM, ai, enm, Wr = [place(n, [P, P]) for n in
            "gi gf li fr lf Bc Ac CM nM ai enm Wr".split()]
        invt = place("invt", [P, 4, GRID_H + GRID_W + CTX], cs_at)
        onesr = place("onesr", [P, P])
        assert top[0] <= nc.sbuf_usable_end, (top[0], nc.sbuf_usable_end)
        mixhi = place("mixhi", [P, KT, T], M0, F32R)
        mixlo = place("mixlo", [P, KT, T], M0 + big, F32R)
        top[0] = M0 + 2 * big
        yt = place("yt", [P, 4, DM])
        tb = place("tb", [P, DM])
        lnrows = place("lnrows", [P, 2, DM])
        h2hi = place("h2hi", [P, KT, T], dt=F32R)
        h2lo = place("h2lo", [P, KT, T], dt=F32R)
        gs = place("gs", [P, T])
        grows = place("grows", [P, 2, DM], top[0] - 4 * T)
        acc = place("acc", [P, T])
        hm2 = place("hm2", [P, KT, P])
        assert top[0] <= nc.sbuf_usable_end, (top[0], nc.sbuf_usable_end)
        u = place("u", [P, FT, T], M0)
        top[0] = M0 + 4 * FT * T
        ushi = place("ushi", [P, 2, GN], dt=F32R)
        uslo = place("uslo", [P, 2, GN], dt=F32R)
        zt = place("zt", [P, 4, DM])
        zb = place("zb", [P, DM])
        grows2 = place("grows2", [P, 2, DM])
        lnrows2 = place("lnrows2", [P, 2, DM])

        ps = stack.enter_context(nc.psum_tensor("ps", [P, 8, 512], F32))

        raw_in = [sem(f"raw_in{b}") for b in range(RAWN)]
        whi_ready, wlo_dve, wlo_pool, pe_unit = sem("whi_ready"), sem("wlo_dve"), sem("wlo_pool"), sem("pe_unit")
        dve_chain, act_chain, pool_chain = sem("dve_chain"), sem("act_chain"), sem("pool_chain")
        rows_in, rowsd_in, bg_in, wg_in = sem("rows_in"), sem("rowsd_in"), sem("bg_in"), sem("wg_in")
        inv_in, m0_in, wpl_in, cs_in = sem("inv_in"), sem("m0_in"), sem("wpl_in"), sem("cs_in")
        x_in = [sem(f"x_in{b}") for b in range(3)]
        ada1_in = [sem(f"ada1_in{b}") for b in range(ADA1_RING)]
        arow_ready, pe_adaT, graw_ready = sem("arow_ready"), sem("pe_adaT"), sem("graw_ready")
        ada_in = [sem(f"ada_in{b}") for b in range(2)]
        ident_ready, consts_ready, rows_silu = sem("ident_ready"), sem("consts_ready"), sem("rows_silu")
        pe_rows, cols_ready, pe_ada, ada_a, ada_b = sem("pe_rows"), sem("cols_ready"), sem("pe_ada"), sem("ada_a"), sem("ada_b")
        var_ready, rstd_ready, xn_ready, pe_xT = sem("var_ready"), sem("rstd_ready"), sem("xn_ready"), sem("pe_xT")
        hm_act, hm_dve, h1hi_ready, h1lo_ready = sem("hm_act"), sem("hm_dve"), sem("h1hi_ready"), sem("h1lo_ready")
        wghi_ready, wglo_ready, pe_gate, gates_ready = sem("wghi_ready"), sem("wglo_ready"), sem("pe_gate"), sem("gates_ready")
        pe_gT, f_abs, ln_ready, rows_ready, pe_grow = sem("pe_gT"), sem("f_abs"), sem("ln_ready"), sem("rows_ready"), sem("pe_grow")
        mrow_ready, pe_mcol, exps_in, exps_ready, pe_tok, tok_ready = (sem("mrow_ready"), sem("pe_mcol"), sem("exps_in"),
            sem("exps_ready"), sem("pe_tok"), sem("tok_ready"))
        rows_out = sem("rows_out")
        tile_out, conv_done, silu_done = sem("tile_out"), sem("conv_done"), sem("silu_done")
        pool_y, pe_v, v_ready, pe_pool, po_ready = sem("pool_y"), sem("pe_v"), sem("v_ready"), sem("pe_pool"), sem("po_ready")
        po_out = [sem("po_out0"), sem("po_out1")]
        both = range(2)
        dm_in = [[sem(f"dm_in{p}{d}") for d in both] for p in both]
        qa_in = [sem(f"qa_in{d}") for d in both]
        d_added, d_exp, d_sel, qa_ready = ([sem(f"{n}{d}") for d in both] for n in ("d_added", "d_exp", "d_sel", "qa_ready"))
        pe_s, p_ready, pe_kt, kw_ready = ([sem(f"{n}{d}") for d in both] for n in ("pe_s", "p_ready", "pe_kt", "kw_ready"))
        pe_num, num_used, pe_u, u_used = ([sem(f"{n}{d}") for d in both] for n in ("pe_num", "num_used", "pe_u", "u_used"))
        hvar_ready, hrstd_ready, hn_ready, pe_hT, hT_used = (sem("hvar_ready"), sem("hrstd_ready"), sem("hn_ready"),
            sem("pe_hT"), sem("hT_used"))
        state_out = sem("state_out")
        pool_back, sig_ready, ml_ready = sem("pool_back"), sem("sig_ready"), sem("ml_ready")
        mixhi_ready, mixlo_ready = sem("mixhi_ready"), sem("mixlo_ready")
        pe_grows, grows_ready, ln_in = sem("pe_grows"), sem("grows_ready"), sem("ln_in")
        y_in = [sem(f"y_in{b}") for b in range(4)]
        pe_out, out_used, t_added = sem("pe_out"), sem("out_used"), sem("t_added")
        lvar, lrstd, lnorm, x1_ready = sem("lvar"), sem("lrstd"), sem("lnorm"), sem("x1_ready")
        y_out = [sem(f"y_out{b}") for b in range(4)]
        tb_ready, pe_yT, hm2_act, hm2_dve, h2hi_ready, h2lo_ready = (sem("tb_ready"), sem("pe_yT"), sem("hm2_act"),
            sem("hm2_dve"), sem("h2hi_ready"), sem("h2lo_ready"))
        g_out, conv_step, conv_ready, gelu_ready, u_ready = (sem("g_out"), sem("conv_step"), sem("conv_ready"),
            sem("gelu_ready"), sem("u_ready"))
        ushi_ready, uslo_ready = sem("ushi_ready"), sem("uslo_ready")
        pe_grows2, grows2_ready, ln2_in = sem("pe_grows2"), sem("grows2_ready"), sem("ln2_in")
        down_used, z_ready = sem("down_used"), sem("z_ready")

        def chain(engine, semaphore):
            count = [0]

            def link(ins):
                count[0] += 1
                ins.then_inc(semaphore, 1)
                engine.wait_ge(semaphore, count[0])
            return link

        def x_rows(x_s, x_p, t):
            return x_s[0, t * P:(t + 1) * P, :] if t < LT else x_p[0, :, :]

        def who(t):
            return int(t >= LT)

        def bc(ap, shape):
            return ap.to_broadcast(shape)

        def times(b):
            return len(range(b, NT, 4))

        def grp(g):
            return slice(g * GN, (g + 1) * GN)

        def chunk(t):
            return slice(t * P, (t + 1) * P)

        def scan_chunks(s):
            return (s, LT - 1 - s) if s < LT else (LT, LT)

        def row0(d, ck):
            return DIR * d + ck

        def rows_of(d, ck):
            return slice(row0(d, ck), row0(d, ck) + NT * (H - 1) + 1, NT)

        NSTEP = NT

        def out_bank(g, i):
            return (2 * GT * g + i) % 8

        def raw_wait(eng, n):
            eng.wait_ge(raw_in[n % RAWN], 16 * (n // RAWN + 1))

        final = [(s, ck) for s in range(LT // 2, LT) for ck in scan_chunks(s)] + [(LT, LT)]

        block = stack.enter_context(nc.Block())

        @block.sync
        def _(sp):
            for src, r in ((c.rearrange("a (r f) -> (a r) f", f=P), V_C),
                           (c_ctx.rearrange("(r f) -> r f", f=P), V_CC),
                           (b_ada.rearrange("a (r f) -> (a r) f", f=P), V_BADA),
                           (hn_g.rearrange("a (r f) -> (a r) f", f=P), V_HN),
                           (pool_scale.rearrange("a (r f) -> (a r) f", f=P), V_PS),
                           (w_qk_conv.rearrange("a t (r f) -> (a t r) f", f=P), V_CONV),
                           (b_dw.rearrange("a (r f) -> (a r) f", f=P), V_BDW)):
                sp.dma_start(rowsv[r:r + src.shape[0], :], src).then_inc(rows_in, 16)
            ada_v = w_ada[0].rearrange("(k p) n -> p k n", p=P)

            def load_ada1(i):
                if i >= ADA1_RING:
                    sp.wait_ge(pe_ada, i - ADA1_RING + 1)
                sp.dma_start(adaw1[:, i % ADA1_RING, :, :], ada_v[:, :, i * AC:(i + 1) * AC]
                             ).then_inc(ada1_in[i % ADA1_RING], 16)

            def load_x0(t):
                if t >= 3:
                    sp.wait_ge(x_in[t % 3], 16 * (t // 3))
                sp.dma_start(xt[:, t, :], x_rows(x_sample, x_prompt, t)).then_inc(x_in[t % 3], 16)

            load_ada1(0)
            load_ada1(1)
            load_x0(0)
            load_ada1(2)
            load_x0(1)
            load_ada1(3)
            load_x0(2)
            load_ada1(4)
            load_ada1(5)
            taps_v = w_dw[0].rearrange("a b (f e) -> (a b f) e", e=P)
            for j in range(2):
                sp.dma_start(rowsd[0:NTAP * FT // 2, j, :],
                             taps_v[j * NTAP * FT // 2:(j + 1) * NTAP * FT // 2, :]).then_inc(rowsd_in, 16)
            sp.dma_start(wgr[:, :, :], w_in[0, :, 5 * H * P:5 * H * P + NGATE].rearrange("(k p) n -> p k n", p=P)
                         ).then_inc(wg_in, 16)
            load_ada1(6)
            load_x0(3)
            load_ada1(7)
            for t in range(4, NT):
                load_x0(t)
            sp.dma_start(bgate[:, :], b_gates[0].partition_broadcast(P)).then_inc(bg_in, 16)

            proj_v = w_in[0].rearrange("(k p) n -> p k n", p=P)

            def load_proj(n):
                if n >= RAWN:
                    m = n - RAWN
                    if m < U_C:
                        sp.wait_ge(wlo_dve, m + 1)
                    else:
                        sp.wait_ge(wlo_pool, m - U_C + 1)
                col = proj_col(n // 2)
                sp.dma_start(raw[:, n % RAWN, :].rearrange("p (k n) -> p k n", k=KT // 2),
                             proj_v[:, (n % 2) * KT // 2:(n % 2 + 1) * KT // 2, col:col + P]
                             ).then_inc(raw_in[n % RAWN], 16)

            for n in range(RAWN):
                load_proj(n)
            sp.dma_start(m0row[:, :], state_m[0].rearrange("a d h -> a (d h)")).then_inc(m0_in, 16)
            sp.dma_start(invt[:, :, :], inv_count.partition_broadcast(P)).then_inc(inv_in, 16)
            sp.wait_ge(pe_xT, NT)
            sp.wait_ge(h1lo_ready, NT)
            sp.dma_start(wpl[:, :, :], w_pool[0].rearrange("g c d -> c g d")).then_inc(wpl_in, 16)
            po_n = 0

            def spill_pool():
                nonlocal po_n
                g, r = po_n // 3, po_n % 3
                sp.wait_ge(po_ready, po_n + 1)
                sp.dma_start(pool_out[:, g, grp(r)], po[:, po_n % 2, :]).then_inc(po_out[po_n % 2], 16)
                po_n += 1

            for n in range(2 * NPROJ):
                if n >= 2:
                    sp.wait_ge(pe_ada, N_ADA1 + n - 1)
                blk = N_ADA1 + n // 2
                sp.dma_start(adaw[:, n % 2, :, :], ada_v[:, (n % 2) * KT // 2:(n % 2 + 1) * KT // 2, blk * AC:(blk + 1) * AC]
                             ).then_inc(ada_in[n % 2], 16)
                if n + RAWN < U_OUT:
                    load_proj(n + RAWN)
                if n == 12:
                    sp.wait_ge(exps_ready, 1)
                    sp.dma_start(scan_rows[0], nM[:, :]).then_inc(rows_out, 16)
                    sp.dma_start(scan_rows[1], ai[:, :]).then_inc(rows_out, 16)
                    for d in both:
                        sp.dma_start(new_m[0, 0, d].rearrange("(h a) -> h a", a=1),
                                     gcol[rows_of(d, LT), 3:4]).then_inc(state_out, 16)
                if n >= 23:
                    spill_pool()

            def scan_load(s):
                for d in both:
                    if s >= 2:
                        sp.wait_ge(pe_num[d], 2 * (s - 1))
                    sp.dma_start(Dm[:, s % 2, d, :, :], scan_rows[0, rows_of(d, scan_chunks(s)[d]), :].partition_broadcast(P)
                                 ).then_inc(dm_in[s % 2][d], 16)
                if s < LT:
                    for d in both:
                        if s >= 1:
                            sp.wait_ge(pe_num[d], 2 * s)
                        sp.dma_start(Qa[:, d, :, :], scan_rows[1, rows_of(d, scan_chunks(s)[d]), :].partition_broadcast(P)
                                     ).then_inc(qa_in[d], 16)

            sp.wait_ge(rows_out, 32)
            sp.wait_ge(pe_adaT, 2)
            sp.wait_ge(tok_ready, 1)
            sp.wait_ge(pool_y, 4)
            scan_load(0)
            for d in both:
                sp.dma_start(Cs[:, d, :, 0:P], state_C[0, 0, d].rearrange("h k v -> k h v")).then_inc(cs_in, 16)
                sp.dma_start(Cs[:, d, :, P:P + 1],
                             state_n[0, 0, d].rearrange("h (k a) -> k h a", a=1)).then_inc(cs_in, 16)
            while po_n < 12:
                spill_pool()
            for s in range(NSTEP):
                if s + 1 < NSTEP:
                    scan_load(s + 1)
                if 2 * NPROJ + s + RAWN < U_OUT:
                    load_proj(2 * NPROJ + s + RAWN)

            def load_out(n):
                m = n - RAWN
                sp.wait_ge(wlo_pool, m - U_C + 1)
                j = n - U_OUT
                k, half = (j // 2) % KT, j % 2
                sp.dma_start(raw[:, n % RAWN, :], w_out[0, k * P:(k + 1) * P, half * UC:(half + 1) * UC]
                             ).then_inc(raw_in[n % RAWN], 16)

            for n in range(U_OUT, U_OUT + RAWN):
                load_out(n)
            for b in both:
                sp.wait_ge(po_out[b], 16 * 6)
            for d in both:
                sp.wait_ge(pe_kt[d], NSTEP)
                sp.wait_ge(pe_s[d], NSTEP)
            sp.dma_start(qk[:, H:2 * H, :], pool_out[:, :, :]).then_inc(pool_back, 16)
            for d in both:
                sp.wait_ge(u_used[d], 2 * NSTEP - 2)
                sp.dma_start(new_C[0, 0, d].rearrange("h k v -> k h v"), Cs[:, d, :, 0:P]).then_inc(state_out, 16)
                sp.dma_start(new_n[0, 0, d].rearrange("h (k a) -> k h a", a=1), Cs[:, d, :, P:P + 1]).then_inc(state_out, 16)

            def load_x(t):
                if t >= 4:
                    sp.wait_ge(y_out[t % 4], 16 * (t // 4))
                    sp.wait_ge(tb_ready, t - 3)
                sp.dma_start(yt[:, t % 4, :], x_rows(x_sample, x_prompt, t)).then_inc(y_in[t % 4], 16)

            def store_x1(t):
                sp.wait_ge(x1_ready, t + 1)
                sp.dma_start(x1_rows[t], yt[:, t % 4, :]).then_inc(y_out[t % 4], 16)

            sp.wait_ge(mixlo_ready, 2 * NG)
            sp.dma_start(lnrows[:, 0, :], ln1_g[0].partition_broadcast(P)).then_inc(ln_in, 16)
            sp.dma_start(lnrows[:, 1, :], ln1_b[0].partition_broadcast(P)).then_inc(ln_in, 16)
            for t in range(GT):
                load_x(t)
            for n in range(U_OUT + RAWN, U_UP):
                g, r = divmod(n - U_OUT, 2 * KT)
                if g >= 1 and r == 12:
                    store_x1(GT * g - 3)
                    load_x(GT * g + 1)
                if g >= 1 and r == 14:
                    store_x1(GT * g - 2)
                    load_x(GT * g + 2)
                if g >= 2 and r == 0:
                    store_x1(GT * (g - 1) - 1)
                if g >= 1 and r == 2:
                    load_x(GT * g)
                load_out(n)
            store_x1(GT * (NG - 1) - 1)
            up_v = w_up[0].rearrange("(k p) n -> p k n", p=P)

            def load_up(i, col):
                for q in range(4):
                    sp.wait_ge(wlo_pool, 4 * i + (U_UP + q - RAWN - U_C + 1))
                    unit = up_v[:, (q % 2) * KT // 2:(q % 2 + 1) * KT // 2, bass.ds(col + (FF if q < 2 else 0), P)]
                    sp.dma_start(raw[:, q, :].rearrange("p (k n) -> p k n", k=KT // 2), unit).then_inc(raw_in[q], 16)

            load_up(0, 0)
            for t in range(NT - GT, NT):
                store_x1(t)
            with sp.Fori(0, FT - 1) as before:
                load_up(before + 1, P * before + P)

            def load_down(g, pair):
                rows2 = [bass.ds(pair * 2 * P + b * P, P) for b in both]
                for q in range(4):
                    unit = w_down[0, rows2[q // 2], (q % 2) * UC:(q % 2 + 1) * UC]
                    sp.wait_ge(wlo_pool, 4 * pair + (U_DOWN + g * 2 * FT + q - RAWN - U_C + 1))
                    sp.dma_start(raw[:, q, :], unit).then_inc(raw_in[q], 16)

            load_down(0, 0)
            sp.wait_ge(pe_unit, U_DOWN)
            sp.dma_start(lnrows2[:, 0, :], ln2_g[0].partition_broadcast(P)).then_inc(ln2_in, 16)
            sp.dma_start(lnrows2[:, 1, :], ln2_b[0].partition_broadcast(P)).then_inc(ln2_in, 16)
            for b in range(4):
                sp.wait_ge(y_out[b], 16 * times(b))
            for t in range(GT):
                sp.dma_start(zt[:, t % 4, :], x1_rows[t]).then_inc(y_in[t % 4], 16)

            def store_y(t):
                sp.wait_ge(z_ready, t + 1)
                sp.dma_start(x_rows(y_sample, y_prompt, t), zt[:, t % 4, :]).then_inc(y_out[t % 4], 16)

            for g in range(NG):
                if g > 0:
                    load_down(g, 0)
                with sp.Fori(1, 7) as pair:
                    load_down(g, pair)
                if g > 0:
                    for i in range(GT):
                        store_y((g - 1) * GT + i)
                    for i in range(GT):
                        t = g * GT + i
                        if t >= 4:
                            sp.wait_ge(y_out[t % 4], 16 * (t // 4 + times(t % 4)))
                        sp.dma_start(zt[:, t % 4, :], x1_rows[t]).then_inc(y_in[t % 4], 16)
                with sp.Fori(7, FT // 2) as pair:
                    load_down(g, pair)
            for i in range(GT):
                store_y((NG - 1) * GT + i)
            for b in range(4):
                sp.wait_ge(y_out[b], 16 * 2 * times(b))
            sp.wait_ge(state_out, 96)

        @block.tensor
        def _(pe):
            mm = nc.tensor.matmul
            pe.wait_ge(ident_ready, 2)
            pe.wait_ge(rows_silu, 1)
            nc.tensor.transpose(ps[:, 7, 0:NV], rowsv[0:NV, :], ident[0:NV, 0:NV]).then_inc(pe_rows, 1)

            def x_transposes(t):
                pe.wait_ge(xn_ready, t + 1)
                if t >= 3:
                    pe.wait_ge(hm_act, t - 2)
                    pe.wait_ge(hm_dve, t - 2)
                for k in range(KT):
                    last = nc.tensor.transpose(ps[:, 2 * (t % 3) + k // 4, (k % 4) * P:(k % 4 + 1) * P],
                                               xt[:, t, k * P:(k + 1) * P], ident[:, :])
                last.then_inc(pe_xT, 1)

            n_half = NTAP * FT // 2
            def ada_mm(k, w):
                return mm(ps[0:2, 6, ADA_AT:ADA_AT + AC], colv[:, V_C + k:V_CC + k + 1:V_CC - V_C], w,
                          start=(k == 0), stop=(k == KT - 1))

            def ada_transposes(j):
                pe.wait_ge(arow_ready, j + 1)
                for b in range(AC // P):
                    blk = j * AC // P + b
                    last = nc.tensor.transpose(ps[:, 6, 2 * blk:2 * blk + 2], arow[:, j % 2, b * P:(b + 1) * P],
                                               ident[0:2, 0:2])
                return last

            pe.wait_ge(cols_ready, 1)
            for i in range(N_ADA1):
                if i >= 1:
                    ada_transposes(i - 1)
                if i in (3, 5, 7):
                    x_transposes((i - 3) // 2)
                if i == 6:
                    pe.wait_ge(rowsd_in, 32)
                    for j in range(2):
                        last = nc.tensor.transpose(ps[:, 7, P * (j + 1):P * (j + 1) + n_half], rowsd[0:n_half, j, :],
                                                   ident[0:n_half, 0:n_half])
                    last.then_inc(pe_rows, 1)
                pe.wait_ge(ada1_in[i % ADA1_RING], 16 * (i // ADA1_RING + 1))
                for k in range(KT):
                    last = ada_mm(k, adaw1[:, i % ADA1_RING, k, :])
                last.then_inc(pe_ada, 1)
            ada_transposes(N_ADA1 - 1).then_inc(pe_adaT, 1)

            def gate_group(g):
                pe.wait_ge(h1lo_ready, GT * (g + 1))
                if g >= 1:
                    pe.wait_ge(graw_ready, g)
                for k in range(KT):
                    for a, b in ((wghi, h1hi), (wghi, h1lo), (wglo, h1hi)):
                        last = mm(ps[0:NGATE, 7, 0:GN], a[:, k, :], b[:, k, grp(g)],
                                  start=(k == 0 and a is wghi and b is h1hi), stop=(k == KT - 1 and a is wglo))
                last.then_inc(pe_gate, 1)

            for t in range(3, 6):
                x_transposes(t)
            pe.wait_ge(wglo_ready, 1)
            pe.wait_ge(cols_ready, 2)
            gate_group(0)
            for t in range(6, NT):
                x_transposes(t)
            gate_group(1)

            def gate_transposes():
                pe.wait_ge(graw_ready, NG)
                for t in range(NT):
                    last = nc.tensor.transpose(ps[:, 7, t * NGATE:(t + 1) * NGATE], graw[:, chunk(t)],
                                               ident[0:NGATE, 0:NGATE])
                last.then_inc(pe_gate, 1)

            def proj_group(n, bank, g):
                for k in range(KT // 2):
                    kk = (n % 2) * KT // 2 + k
                    for a, b in ((whi, h1hi), (whi, h1lo), (wlo, h1hi)):
                        last = mm(ps[:, bank, 0:GN], a[:, n % 2, k * P:(k + 1) * P], b[:, kk, grp(g)],
                                  start=(kk == 0 and a is whi and b is h1hi), stop=(kk == KT - 1 and a is wlo))
                return last

            jobs_done = {"v": 0, "pool": 0}

            def misc_job(job):
                kind = job[0]
                if kind == "gT":
                    pe.wait_ge(gates_ready, 1)
                    nc.tensor.transpose(ps[:, 7, 0:P], gi[:, :], ident[:, :])
                    nc.tensor.transpose(ps[:, 7, P:2 * P], gf[:, :], ident[:, :]).then_inc(pe_gT, 1)
                elif kind == "grow":
                    pe.wait_ge(rows_ready, 1)
                    for j in range(2):
                        last = mm(ps[0:1, 7, j * P:(j + 1) * P], gcol[:, j:j + 1], ident[:, :], start=True, stop=True)
                    last.then_inc(pe_grow, 1)
                elif kind == "mcol":
                    pe.wait_ge(mrow_ready, 1)
                    mm(ps[:, 7, 0:1], mrow[0:1, :], one11[0:1, :], start=True, stop=True).then_inc(pe_mcol, 1)
                elif kind == "tok":
                    pe.wait_ge(exps_ready, 1)
                    for j, src in enumerate((Ac, Wr, enm)):
                        nc.tensor.transpose(ps[:, 7, j * P:(j + 1) * P], src[:, :], ident[:, :])
                    mm(ps[:, 7, 3 * P:4 * P], bc(gcol[:, 4:5], [P, P]), ident[:, :], start=True, stop=True).then_inc(pe_tok, 1)
                elif kind == "v":
                    _, h, part = job
                    pe.wait_ge(tok_ready, 1)
                    pe.wait_ge(tile_out, H + h + 1)
                    if jobs_done["v"]:
                        pe.wait_ge(v_ready, jobs_done["v"] + 1)
                    for ck in range(4 * part, min(4 * part + 4, NT)):
                        last = nc.tensor.transpose(ps[:, 7, (ck % 4) * P:(ck % 4 + 1) * P], qk[:, h, chunk(ck)], ident[:, :])
                    last.then_inc(pe_v, 1)
                    jobs_done["v"] += 1
                elif kind == "pool":
                    _, g, part = job
                    pe.wait_ge(v_ready, 13)
                    pe.wait_ge(wpl_in, 16)
                    pe.wait_ge(pool_y, g + 1)
                    if jobs_done["pool"]:
                        pe.wait_ge(po_ready, jobs_done["pool"])
                    mm(ps[:, 7, 0:GN], wpl[:, g, :], qk[:, H + g, grp(part)], start=True, stop=True).then_inc(pe_pool, 1)
                    jobs_done["pool"] += 1

            for n in range(2 * NPROJ):
                tile, bank = n // 2, 3 * ((n // 2) % 2)
                pe.wait_ge(wlo_dve, n + 1)
                if n == 2:
                    pe.wait_ge(hm_act, NT)
                    pe.wait_ge(hm_dve, NT)
                if n % 2 == 0 and tile >= 2:
                    pe.wait_ge(tile_out, tile - 1)
                for g in range(NG):
                    if n == 0 and g == 0:
                        pe.wait_ge(hm_act, 7)
                        pe.wait_ge(hm_dve, 7)
                    if n == 0 and g == 2:
                        gate_group(2)
                        pe.wait_ge(hm_act, 8)
                        pe.wait_ge(hm_dve, 8)
                    last = proj_group(n, bank + g, g)
                last.then_inc(pe_unit, 1)
                pe.wait_ge(ada_in[n % 2], 16 * (n // 2 + 1))
                if n and n % 2 == 0:
                    ada_transposes(N_ADA1 + n // 2 - 1)
                for k in range(KT // 2):
                    last = ada_mm((n % 2) * KT // 2 + k, adaw[:, n % 2, k, :])
                last.then_inc(pe_ada, 1)
                if n == 0:
                    gate_transposes()
                if n in JOBS:
                    misc_job(JOBS[n])
            for job in LATE_JOBS:
                misc_job(job)
            ada_transposes(N_ADA - 1).then_inc(pe_adaT, 1)

            def scores(s, d):
                ck = scan_chunks(s)[d]
                if s == 0:
                    pe.wait_ge(silu_done, 2 * H)
                    pe.wait_ge(tile_out, NPROJ)
                else:
                    pe.wait_ge(p_ready[d], s)
                for h in range(H):
                    last = mm(ps[:, 3 + d, h * P:(h + 1) * P], qk[:, H + h, chunk(ck)], qk[:, h, chunk(ck)],
                              start=True, stop=True)
                last.then_inc(pe_s[d], 1)

            def k_transposes(s, d):
                ck = scan_chunks(s)[d]
                if d == 1:
                    pe.wait_ge(kw_ready[0], s + 1)
                elif s >= 1:
                    pe.wait_ge(kw_ready[1], s)
                    if hT[0]:
                        pe.wait_ge(hT_used, hT[0])
                for h in range(H):
                    last = nc.tensor.transpose(ps[:, 5, h * P:(h + 1) * P], qk[:, H + h, chunk(ck)], ident[:, :])
                last.then_inc(pe_kt[d], 1)

            def numerators(s, d):
                ck = scan_chunks(s)[d]
                pe.wait_ge(p_ready[d], s + 1)
                if s < LT:
                    pe.wait_ge(qa_ready[d], s + 1)
                    if s == 0:
                        pe.wait_ge(cs_in, 64)
                        pe.wait_ge(ada_b, 1)
                        pe.wait_ge(po_ready, 12)
                    elif s >= 1:
                        pe.wait_ge(u_used[d], 2 * s)
                if d == 1:
                    pe.wait_ge(num_used[0], 2 * s + 2)
                elif s >= 1:
                    pe.wait_ge(u_used[1] if s < LT else num_used[1], 2 * s)
                for pair in range(2):
                    for hh in range(2):
                        h = 2 * pair + hh
                        out = ps[:, 6 + pair, hh * (P + 1):(hh + 1) * (P + 1)]
                        last = mm(out, Dm[:, s % 2, d, h, :], v1[:, ck, h, :], start=True, stop=(s == LT))
                        if s < LT:
                            last = mm(out, Qa[:, d, h, :], Cs[:, d, h, :], start=False, stop=True)
                    last.then_inc(pe_num[d], 1)

            def updates(s, d):
                ck = scan_chunks(s)[d]
                pe.wait_ge(kw_ready[d], s + 1)
                if d == 0:
                    pe.wait_ge(num_used[1], 2 * s + 2)
                else:
                    pe.wait_ge(u_used[0], 2 * s + 2 if s < LT else 2 * s)
                for pair in range(2):
                    for hh in range(2):
                        h = 2 * pair + hh
                        last = mm(ps[:, 6 + pair, hh * (P + 1):(hh + 1) * (P + 1)], kw[:, d, h, :], v1[:, ck, h, :],
                                  start=True, stop=True)
                    last.then_inc(pe_u[d], 1)

            hT = [0]

            def h_transposes(ck):
                pe.wait_ge(hn_ready, hT[0] + 1)
                if hT[0]:
                    pe.wait_ge(hT_used, hT[0])
                pe.wait_ge(kw_ready[1], min(final[hT[0]][0] + 2, NSTEP))
                for h in range(H):
                    last = nc.tensor.transpose(ps[:, 5, h * P:(h + 1) * P], hacc[:, ck, h, :], ident[:, :])
                last.then_inc(pe_hT, 1)
                hT[0] += 1

            for s in range(NSTEP):
                n = U_C + s

                def slot(g):
                    if n < U_OUT:
                        if g == 0:
                            pe.wait_ge(wlo_pool, s + 1)
                            if s % 2 == 0:
                                pe.wait_ge(tile_out, NPROJ + s // 2)
                        last = proj_group(n, g, g)
                        if g == NG - 1:
                            last.then_inc(pe_unit, 1)

                scores(s, 0)
                scores(s, 1)
                k_transposes(s, 0)
                if 1 <= s < LT:
                    updates(s - 1, 1)
                slot(0)
                k_transposes(s, 1)
                numerators(s, 0)
                slot(1)
                done = [ck for at, ck in final if at == s - 1]
                numerators(s, 1)
                for ck in done[:1]:
                    h_transposes(ck)
                slot(2)
                if s != LT - 1:
                    updates(s, 0)
                for ck in done[1:]:
                    h_transposes(ck)
            updates(LT, 1)
            pe.wait_ge(tile_out, NPROJ + H)
            for w in both:
                for k in range(KT):
                    last = mm(ps[:, 2 * w + k // 4, (k % 4) * P:(k % 4 + 1) * P],
                              bc(adaT[:, A_G1 + k, w:w + 1], [P, P]), ident[:, :], start=True, stop=True)
            last.then_inc(pe_grows, 1)
            h_transposes(LT)

            def y_transposes(t, g):
                bank = out_bank(g, 2 * GT)
                pe.wait_ge(tb_ready, t + 1)
                pe.wait_ge(out_used, 2 * GT * (t // GT + 1))
                if t >= 1:
                    pe.wait_ge(hm2_act, t)
                    pe.wait_ge(hm2_dve, t)
                for k in range(KT):
                    last = nc.tensor.transpose(ps[:, bank + k // 4, (k % 4) * P:(k % 4 + 1) * P],
                                               tb[:, k * P:(k + 1) * P], ident[:, :])
                last.then_inc(pe_yT, 1)

            pe.wait_ge(grows_ready, 1)
            pe.wait_ge(hT_used, NT)
            pe.wait_ge(p_ready[1], NSTEP)
            for g in range(NG):
                pe.wait_ge(mixhi_ready, 2 * (g + 1))
                pe.wait_ge(mixlo_ready, 2 * (g + 1))
                for k in range(KT):
                    for half in range(2):
                        n = U_OUT + (g * KT + k) * 2 + half
                        pe.wait_ge(wlo_pool, n - U_C + 1)
                        for i in range(GT):
                            bank = out_bank(g, 2 * i + half)
                            if k == 0:
                                before = 2 * GT * g + 2 * i + half - 8
                                if before >= 0:
                                    pe.wait_ge(out_used, before + 1)
                                if g == 1 and i == 0:
                                    pe.wait_ge(u_used[1], 2 * NSTEP - 2)
                                if g == 2 and i == 0:
                                    pe.wait_ge(hm2_act, GT)
                                    pe.wait_ge(hm2_dve, GT)
                            for a, b in ((mixhi, whi), (mixhi, wlo), (mixlo, whi)):
                                last = mm(ps[:, bank, :], a[:, k, chunk(g * GT + i)], b[:, n % 2, :],
                                          start=(k == 0 and a is mixhi and b is whi), stop=(k == KT - 1 and a is mixlo))
                        last.then_inc(pe_unit, 1)
                    if g >= 1 and k >= 5:
                        y_transposes((g - 1) * GT + k - 5, g)
            for i in range(GT):
                y_transposes((NG - 1) * GT + i, NG - 1)

            def up_tile(i, first=False):
                for q in range(4):
                    pe.wait_ge(wlo_pool, 4 * i + (U_UP + q - U_C + 1))
                    if q == 0:
                        if first:
                            pe.wait_ge(out_used, 2 * NT)
                            pe.wait_ge(hm2_act, NT)
                            pe.wait_ge(hm2_dve, NT)
                        else:
                            pe.wait_ge(g_out, i)
                    if q == 2 and not first:
                        pe.wait_ge(u_ready, i)
                    for g in range(NG):
                        if first and q == 0:
                            pe.wait_ge(h2lo_ready, GT * (g + 1))
                        for k in range(KT // 2):
                            kk = (q % 2) * KT // 2 + k
                            for a, b in ((whi, h2hi), (whi, h2lo), (wlo, h2hi)):
                                last = mm(ps[:, 3 * (q // 2) + g, 0:GN], a[:, q % 2, k * P:(k + 1) * P], b[:, kk, grp(g)],
                                          start=(kk == 0 and a is whi and b is h2hi), stop=(kk == KT - 1 and a is wlo))
                    last.then_inc(pe_unit, 1)

            up_tile(0, first=True)
            with pe.Fori(1, FT) as i:
                up_tile(i)

            def down_pair(g, pair, first=False, final_pair=False):
                for q in range(4):
                    pe.wait_ge(wlo_pool, 4 * pair + (U_DOWN + g * 2 * FT + q - U_C + 1))
                    if q % 2 == 0:
                        pe.wait_ge(uslo_ready, 2 * pair + (g * FT + q // 2 + 1))
                    for i in range(GT):
                        bank = out_bank(g, 2 * i + q % 2)
                        if first and q < 2:
                            if g >= 1:
                                before = 2 * GT * g + 2 * i + q % 2 - 8
                                if before >= 0:
                                    pe.wait_ge(down_used, before + 1)
                                if g == 1 and i == 0:
                                    pe.wait_ge(grows2_ready, 2)
                            else:
                                pe.wait_ge(u_ready, FT)
                                pe.wait_ge(g_out, FT)
                        for a, b in ((ushi, whi), (ushi, wlo), (uslo, whi)):
                            last = mm(ps[:, bank, :], a[:, q // 2, i * P:(i + 1) * P], b[:, q % 2, :],
                                      start=(first and q < 2 and a is ushi and b is whi),
                                      stop=(final_pair and q >= 2 and a is uslo))
                    last.then_inc(pe_unit, 1)

            for g in range(NG):
                down_pair(g, 0, first=True)
                if g == 0:
                    for w in both:
                        if w:
                            pe.wait_ge(grows2_ready, 1)
                        for k in range(KT):
                            last = mm(ps[:, 6 + k // 4, (k % 4) * P:(k % 4 + 1) * P],
                                      bc(adaT[:, A_G2 + k, w:w + 1], [P, P]), ident[:, :], start=True, stop=True)
                        last.then_inc(pe_grows2, 1)
                with pe.Fori(1, FT // 2 - 1) as pair:
                    down_pair(g, pair)
                down_pair(g, FT // 2 - 1, final_pair=True)

        @block.scalar
        def _(act):
            link = chain(act, act_chain)
            fn = nc.scalar.activation

            def hi(n):
                raw_wait(act, n)
                if n >= 2:
                    act.wait_ge(pe_unit, n - 1)
                fn(whi[:, n % 2, :], raw[:, n % RAWN, :], ACT.Copy).then_inc(whi_ready, 1)

            act.wait_ge(rows_in, 7 * 16)
            fn(rowsv[0:V_BADA, :], rowsv[0:V_BADA, :], ACT.Silu).then_inc(rows_silu, 1)
            act.wait_ge(pe_rows, 1)
            fn(colv[:, :], ps[:, 7, 0:NV], ACT.Copy).then_inc(cols_ready, 1)
            half = NTAP * FT // 2
            for i in range(N_ADA1):
                if i == 6:
                    act.wait_ge(pe_rows, 2)
                    fn(dwc[:, :].rearrange("p (j n) -> p j n", j=2),
                       ps[:, 7, P:3 * P].rearrange("p (j n) -> p j n", j=2)[:, :, 0:half], ACT.Copy).then_inc(cols_ready, 1)
                    act.wait_ge(wg_in, 16)
                    fn(wghi[:, :, :], wgr[:, :, :], ACT.Copy).then_inc(wghi_ready, 1)
                act.wait_ge(pe_ada, i + 1)
                fn(arow[:, i % 2, :], ps[0:2, 6, ADA_AT:ADA_AT + AC], ACT.Copy).then_inc(arow_ready, 1)
            act.wait_ge(ada_a, 1)
            for t in range(NT):
                act.wait_ge(pe_xT, t + 1)
                if t >= 2:
                    act.wait_ge(h1lo_ready, t - 1)
                w = who(t)
                for k in range(KT // 2):
                    last = fn(hm[:, t % 2, k, :], ps[:, 2 * (t % 3), k * P:(k + 1) * P], ACT.Identity,
                              scale=ada1p[:, 0, k, w:w + 1], bias=adaT[:, A_SH1 + k, w:w + 1])
                last.then_inc(hm_act, 1)
                act.wait_ge(hm_act, t + 1)
                act.wait_ge(hm_dve, t + 1)
                fn(h1hi[:, :, chunk(t)], hm[:, t % 2, :, :], ACT.Copy).then_inc(h1hi_ready, 1)
                if t == 4:
                    hi(0)
                    hi(1)

            def po_evac(j):
                act.wait_ge(pe_pool, j + 1)
                if j >= 2:
                    act.wait_ge(po_out[j % 2], 16 * (j // 2))
                g = j // 3
                fn(po[:, j % 2, :], ps[:, 7, 0:GN], ACT.Copy, scale=colv[:, V_PS + g:V_PS + g + 1]).then_inc(po_ready, 1)

            def silu(j):
                act.wait_ge(conv_done, j + 1)
                fn(qk[:, j, :], qk[:, j, :], ACT.Silu).then_inc(silu_done, 1)

            act.wait_ge(h1lo_ready, NT)
            for n in range(2 * NPROJ):
                job = JOBS.get(n - 1, ("",))
                if job[0] == "pool":
                    po_evac(3 * job[1] + job[2])
                hi(n + 2)
                if n % 2:
                    tile = n // 2
                    act.wait_ge(pe_unit, n + 1)
                    if tile < H:
                        dst = qk[:, H + tile, :]
                    elif tile < 2 * H:
                        dst = qk[:, tile - H, :]
                    else:
                        dst = work[:, tile % 2, :]
                        if tile >= 2 * H + 2:
                            act.wait_ge(conv_done, tile - 2 * H - 1)
                    b0 = 3 * (tile % 2)
                    fn(dst.rearrange("p (g n) -> p g n", g=NG), ps[:, b0:b0 + 3, 0:GN], ACT.Copy).then_inc(tile_out, 1)
                    if 2 * H < tile:
                        silu(tile - 2 * H - 1)
                if n == 2:
                    act.wait_ge(f_abs, 1)
                    link(fn(Wr[:, :], lf[:, :], ACT.Exp, scale=-1.0))
                    fn(Wr[:, :], Wr[:, :], ACT.Ln, bias=1.0).then_inc(ln_ready, 1)
                if n == 7:
                    act.wait_ge(exps_in, 1)
                    fn(ai[:, :], nM[:, :], ACT.Exp, bias=gcol[:, 2:3])
                    fn(enm[:, :], enm[:, :], ACT.Exp)
                    fn(gcol[:, 4:5], gcol[:, 4:5], ACT.Exp)
                    fn(Wr[:, :], Ac[:, :], ACT.Exp, bias=gcol[:, 5:6]).then_inc(exps_ready, 1)
            po_evac(9)
            po_evac(10)
            po_evac(11)
            silu(2 * H - 1)

            def d_exps(s, d):
                act.wait_ge(d_added[d], s + 1)
                D = Dm[:, s % 2, d, :, :]
                fn(D, D, ACT.Exp).then_inc(d_exp[d], 1)

            fin = [0]

            def h_evac():
                ck = final[fin[0]][1]
                act.wait_ge(pe_hT, fin[0] + 1)
                fn(qk[:, 0:H, chunk(ck)], ps[:, 5, :].rearrange("p (h n) -> p h n", h=H), ACT.Copy).then_inc(hT_used, 1)
                fin[0] += 1

            d_exps(0, 0)
            d_exps(0, 1)
            for s in range(NSTEP):
                n = U_C + s
                if s + 1 < NSTEP:
                    d_exps(s + 1, 0)
                    d_exps(s + 1, 1)
                done = [ck for at, ck in final if at == s - 1]
                if done:
                    h_evac()
                if n < U_OUT:
                    hi(n + 2)
                if done:
                    h_evac()
                if n < U_OUT and s % 2:
                    act.wait_ge(pe_unit, n + 1)
                    fn(work[:, s // 2, :].rearrange("p (g n) -> p g n", g=NG), ps[:, 0:3, 0:GN], ACT.Copy).then_inc(tile_out, 1)
            act.wait_ge(tile_out, NPROJ + H)
            for j in range(H):
                last = fn(work[:, j, :], work[:, j, :], ACT.Sigmoid)
            last.then_inc(sig_ready, 1)
            h_evac()
            act.wait_ge(pe_grows, 1)
            for w in both:
                last = fn(grows[:, w, :].rearrange("p (b n) -> p b n", b=2), ps[:, 2 * w:2 * w + 2, :], ACT.Copy)
            last.then_inc(grows_ready, 1)
            act.wait_ge(pe_unit, U_OUT)
            act.wait_ge(pool_back, 16)
            for g in range(NG):
                fn(mixhi[:, 0:H, grp(g)], qk[:, H:2 * H, grp(g)], ACT.Copy).then_inc(mixhi_ready, 1)
                act.wait_ge(ml_ready, g + 1)
                fn(mixhi[:, H:2 * H, grp(g)], qk[:, 0:H, grp(g)], ACT.Copy).then_inc(mixhi_ready, 1)

            def modulate2(t, bank):
                act.wait_ge(pe_yT, t + 1)
                if t >= 1:
                    act.wait_ge(h2lo_ready, t)
                w = who(t)
                for k in range(KT // 2):
                    last = fn(hm2[:, k, :], ps[:, bank, k * P:(k + 1) * P], ACT.Identity,
                              scale=ada1p[:, 1, k, w:w + 1], bias=adaT[:, A_SH2 + k, w:w + 1])
                last.then_inc(hm2_act, 1)
                act.wait_ge(hm2_act, t + 1)
                act.wait_ge(hm2_dve, t + 1)
                fn(h2hi[:, :, chunk(t)], hm2[:, :, :], ACT.Copy).then_inc(h2hi_ready, 1)

            for g in range(NG):
                for k in range(KT):
                    for half in range(2):
                        hi(U_OUT + (g * KT + k) * 2 + half + 2)
                    if g >= 1 and k >= 5:
                        modulate2((g - 1) * GT + k - 5, out_bank(g, 2 * GT))
            for i in range(GT):
                modulate2((NG - 1) * GT + i, out_bank(NG - 1, 2 * GT))

            def up_tile(i, first=False):
                for q in range(4):
                    m = q + 2
                    act.wait_ge(raw_in[m % 4], 16 * i + 16 * (U_UP // 4 + 1 + m // 4))
                    act.wait_ge(pe_unit, 4 * i + (U_UP + q + 1))
                    fn(whi[:, m % 2, :], raw[:, m % 4, :], ACT.Copy).then_inc(whi_ready, 1)
                    if q == 1:
                        if not first:
                            act.wait_ge(conv_ready, i)
                        fn(gs[:, :].rearrange("p (g n) -> p g n", g=NG), ps[:, 0:3, 0:GN], ACT.Copy).then_inc(g_out, 1)
                act.wait_ge(conv_ready, 1 * i + 1)
                fn(acc[:, :], acc[:, :], ACT.Gelu_apprx_tanh, bias=taps[:, NTAP:NTAP + 1]).then_inc(gelu_ready, 1)

            up_tile(0, first=True)
            with act.Fori(1, FT) as i:
                up_tile(i)

            def down_pair(g, pair, last_pair=False):
                base = U_DOWN + g * 2 * FT
                for q in range(4):
                    if not (last_pair and g == NG - 1 and q >= 2):
                        m = q + 2
                        act.wait_ge(raw_in[m % 4], 16 * pair + 16 * (base // 4 + 1 + m // 4))
                        act.wait_ge(pe_unit, 4 * pair + (base + q + 1))
                        fn(whi[:, m % 2, :], raw[:, m % 4, :], ACT.Copy).then_inc(whi_ready, 1)
                    if q % 2 == 1:
                        if last_pair:
                            if g < NG - 1:
                                fn(ushi[:, q // 2, :], u[:, q // 2, grp(g + 1)], ACT.Copy).then_inc(ushi_ready, 1)
                        else:
                            fn(ushi[:, q // 2, :], u[:, bass.ds(2 * pair + (2 + q // 2), 1), grp(g)], ACT.Copy
                               ).then_inc(ushi_ready, 1)

            act.wait_ge(pe_unit, U_DOWN)
            act.wait_ge(u_ready, FT)
            for b in range(2):
                fn(ushi[:, b, :], u[:, b, grp(0)], ACT.Copy).then_inc(ushi_ready, 1)
            for g in range(NG):
                down_pair(g, 0)
                if g == 0:
                    for w in both:
                        act.wait_ge(pe_grows2, w + 1)
                        fn(grows2[:, w, :].rearrange("p (b n) -> p b n", b=2), ps[:, 6:8, :], ACT.Copy).then_inc(grows2_ready, 1)
                with act.Fori(1, FT // 2 - 1) as pair:
                    down_pair(g, pair)
                down_pair(g, FT // 2 - 1, last_pair=True)

        @block.gpsimd
        def _(pool):
            link = chain(pool, pool_chain)
            nc.gpsimd.memset(ident[:, :], 0.0).then_inc(ident_ready, 1)
            pool.wait_ge(ident_ready, 1)
            nc.gpsimd.affine_select(out=ident[:, :], in_=ident[:, :], compare_op=ALU.not_equal, fill=1.0, base=0,
                                    pattern=[[-1, P]], channel_multiplier=1).then_inc(ident_ready, 1)

            def sub_hi(out, full, hi_part):
                return nc.gpsimd.tensor_tensor(out, full, hi_part.bitcast(F32), ALU.subtract)

            pool.wait_ge(consts_ready, 1)
            for t in range(NT):
                pool.wait_ge(var_ready, t + 1)
                nc.gpsimd.tensor_tensor(rstd[:, t % 4, :], mv[:, t % 4, 1:2], neghalf[:, 0, :], ALU.pow).then_inc(rstd_ready, 1)
                if t == 3:
                    pool.wait_ge(wghi_ready, 1)
                    sub_hi(wglo[:, :, :], wgr[:, :, :], wghi[:, :, :]).then_inc(wglo_ready, 1)
            for t in range(NT):
                pool.wait_ge(h1hi_ready, t + 1)
                sub_hi(h1lo[:, :, chunk(t)], hm[:, t % 2, :, :], h1hi[:, :, chunk(t)]).then_inc(h1lo_ready, 1)

            tt = nc.gpsimd.tensor_tensor
            pool.wait_ge(inv_in, 16)
            pool.wait_ge(pe_ada, N_ADA1)
            for g, win in enumerate(WINDOWS):
                steps = win.bit_length() - 1
                xg = qk[:, H + g, :]
                pool.wait_ge(tile_out, g + 1)
                if g:
                    pool.wait_ge(pool_y, g)
                link(nc.gpsimd.memset(poolA[:, :], 0.0))
                link(nc.gpsimd.tensor_copy(poolA[:, 8 * GRID_W:24 * GRID_W], xg[:, 0:LAT]))
                a, b = poolA, poolB
                for lv in range(1, steps + 1):
                    ext = win // 2 - (1 << (lv - 1))
                    lo_r, n_r = 8 - ext, GRID_H + 2 * ext
                    back, ahead = (1, 0) if lv == 1 else (1 << (lv - 2), 1 << (lv - 2))
                    link(tt(b[:, lo_r * GRID_W:(lo_r + n_r) * GRID_W],
                            a[:, (lo_r - back) * GRID_W:(lo_r - back + n_r) * GRID_W],
                            a[:, (lo_r + ahead) * GRID_W:(lo_r + ahead + n_r) * GRID_W], ALU.add))
                    a, b = b, a
                nlat = GRID_H * PADW
                link(nc.gpsimd.memset(b[:, 0:nlat + PADC], 0.0))

                def padded(buf):
                    return (buf[:, 0:nlat].rearrange("p (r w) -> p r w", w=PADW), buf[:, nlat:nlat + PADC])
                link(nc.gpsimd.tensor_copy(padded(b)[0][:, :, 8:8 + GRID_W],
                                           a[:, 8 * GRID_W:24 * GRID_W].rearrange("p (r w) -> p r w", w=GRID_W)))
                link(nc.gpsimd.tensor_copy(padded(b)[1][:, 8:8 + CTX], xg[:, LAT:T]))
                a, b = b, a
                for lv in range(1, steps + 1):
                    ext = win // 2 - (1 << (lv - 1))
                    back, ahead = (1, 0) if lv == 1 else (1 << (lv - 2), 1 << (lv - 2))
                    at = 8 - ext
                    (al, ac), (bl, bctx) = padded(a), padded(b)
                    for dst, src, n_c in ((bl, al, GRID_W + 2 * ext), (bctx, ac, CTX + 2 * ext)):
                        link(tt(dst[..., at:at + n_c], src[..., at - back:at - back + n_c],
                                src[..., at + ahead:at + ahead + n_c], ALU.add))
                    a, b = b, a
                al, ac = padded(a)
                bl, bctx = padded(b)
                res, xl = al[:, :, 8:8 + GRID_W], xg[:, 0:LAT].rearrange("p (r w) -> p r w", w=GRID_W)
                mid = bl[:, :, 8:8 + GRID_W]
                link(tt(mid, res, bc(invt[:, g, 0:GRID_H].unsqueeze(2), [P, GRID_H, GRID_W]), ALU.mult))
                link(tt(res, mid, bc(invt[:, g, GRID_H:GRID_H + GRID_W].unsqueeze(1), [P, GRID_H, GRID_W]), ALU.mult))
                link(tt(bctx[:, 8:8 + CTX], ac[:, 8:8 + CTX], invt[:, g, GRID_H + GRID_W:], ALU.mult))
                link(tt(xl, res, xl, ALU.subtract))
                tt(xg[:, LAT:T], bctx[:, 8:8 + CTX], xg[:, LAT:T], ALU.subtract).then_inc(pool_y, 1)

            def lo(n):
                pool.wait_ge(whi_ready, n + 1)
                sub_hi(wlo[:, n % 2, :], raw[:, n % RAWN, :], whi[:, n % 2, :]).then_inc(wlo_pool, 1)

            def select(s, d):
                pool.wait_ge(d_exp[d], s + 1)
                D = Dm[:, s % 2, d, :, :]
                sgn = 1 if d == 0 else -1
                nc.gpsimd.affine_select(out=D, in_=D, compare_op=ALU.is_ge, fill=0.0, base=0,
                                        pattern=[[0, H], [sgn, P]], channel_multiplier=-sgn).then_inc(d_sel[d], 1)
                if s < LT:
                    ck = scan_chunks(s)[d]
                    pool.wait_ge(qa_in[d], 16 * (s + 1))
                    if s == 0 and d == 0:
                        pool.wait_ge(silu_done, 2 * H)
                    tt(Qa[:, d, :, :], Qa[:, d, :, :], qk[:, 0:H, chunk(ck)], ALU.mult).then_inc(qa_ready[d], 1)

            fin = 0
            select(0, 0)
            select(0, 1)
            lo(U_C)
            lo(U_C + 1)
            for s in range(NSTEP):
                n_fin = len([ck for at, ck in final if at == s - 1])
                for _ in range(n_fin):
                    pool.wait_ge(hvar_ready, fin + 1)
                    tt(rsh[:, fin % 2, :, :], mvh[:, fin % 2, :, 1:2], neghalf[:, :, :], ALU.pow).then_inc(hrstd_ready, 1)
                    fin += 1
                if s + 1 < NSTEP:
                    select(s + 1, 0)
                    select(s + 1, 1)
                if U_C + s < U_OUT:
                    lo(U_C + s + 2)
            pool.wait_ge(hvar_ready, fin + 1)
            tt(rsh[:, fin % 2, :, :], mvh[:, fin % 2, :, 1:2], neghalf[:, :, :], ALU.pow).then_inc(hrstd_ready, 1)
            for g in range(NG):
                for j, (dst, src) in enumerate(((slice(0, H), slice(H, 2 * H)), (slice(H, 2 * H), slice(0, H)))):
                    pool.wait_ge(mixhi_ready, 2 * g + j + 1)
                    sub_hi(mixlo[:, dst, grp(g)], qk[:, src, grp(g)], mixhi[:, dst, grp(g)]).then_inc(mixlo_ready, 1)

            def rstd_ln(j):
                pool.wait_ge(lvar, j + 1)
                tt(rstd[:, j % 4, :], mv[:, j % 4, 1:2], neghalf[:, 0, :], ALU.pow).then_inc(lrstd, 1)

            def gain(buf, t, rows, norm_sem, count, done):
                pool.wait_ge(norm_sem, count)
                link(tt(buf[:, t % 4, :], buf[:, t % 4, :], rows[:, 0, :], ALU.mult))
                tt(buf[:, t % 4, :], buf[:, t % 4, :], rows[:, 1, :], ALU.add).then_inc(done, 1)

            def h2_lo(t):
                pool.wait_ge(h2hi_ready, t + 1)
                sub_hi(h2lo[:, :, chunk(t)], hm2[:, :, :], h2hi[:, :, chunk(t)]).then_inc(h2lo_ready, 1)

            def gain1(t):
                gain(yt, t, lnrows, lnorm, t + 1, x1_ready)

            pool.wait_ge(ln_in, 32)
            for g in range(NG):
                j0, t0 = 2 * GT * (g - 1), GT * (g - 1)
                for k in range(KT):
                    for half in range(2):
                        lo(U_OUT + (g * KT + k) * 2 + half + 2)
                    if g >= 1:
                        if k == 2:
                            for i in range(GT):
                                rstd_ln(j0 + i)
                        if 4 <= k <= 6:
                            rstd_ln(j0 + GT + k - 4)
                        if 3 <= k <= 5:
                            gain1(t0 + k - 3)
                        if k >= 5:
                            h2_lo(t0 + k - 5)
            j0, t0 = 2 * GT * (NG - 1), GT * (NG - 1)
            for i in range(GT):
                rstd_ln(j0 + i)
            gain1(t0)
            for i in range(GT):
                rstd_ln(j0 + GT + i)
                if i + 1 < GT:
                    gain1(t0 + i + 1)
                h2_lo(t0 + i)

            def up_tile(i):
                for q in range(4):
                    m = q + 2
                    pool.wait_ge(whi_ready, 4 * i + (U_UP + m + 1))
                    sub_hi(wlo[:, m % 2, :], raw[:, m % 4, :], whi[:, m % 2, :]).then_inc(wlo_pool, 1)

            with pool.Fori(0, FT) as i:
                up_tile(i)

            def down_pair(g, pair, last_pair=False):
                base = U_DOWN + g * 2 * FT
                for q in range(4):
                    if not (last_pair and g == NG - 1 and q >= 2):
                        m = q + 2
                        pool.wait_ge(whi_ready, 4 * pair + (base + m + 1))
                        sub_hi(wlo[:, m % 2, :], raw[:, m % 4, :], whi[:, m % 2, :]).then_inc(wlo_pool, 1)
                    if q % 2 == 1 and not (last_pair and g == NG - 1):
                        pool.wait_ge(ushi_ready, 2 * pair + (g * FT + 2 + q // 2 + 1))
                        src = u[:, q // 2, grp(g + 1)] if last_pair else u[:, bass.ds(2 * pair + (2 + q // 2), 1), grp(g)]
                        sub_hi(uslo[:, q // 2, :], src, ushi[:, q // 2, :]).then_inc(uslo_ready, 1)

            def gain2(t):
                gain(zt, t, lnrows2, lnorm, NT + t + 1, z_ready)

            for b in range(2):
                pool.wait_ge(ushi_ready, b + 1)
                sub_hi(uslo[:, b, :], u[:, b, grp(0)], ushi[:, b, :]).then_inc(uslo_ready, 1)
            pool.wait_ge(ln2_in, 32)
            for g in range(NG):
                down_pair(g, 0)
                with pool.Fori(1, 3) as pair:
                    down_pair(g, pair)
                if g >= 1:
                    for i in range(GT):
                        rstd_ln(2 * NT + (g - 1) * GT + i)
                with pool.Fori(3, 5) as pair:
                    down_pair(g, pair)
                if g >= 1:
                    for i in range(GT):
                        gain2((g - 1) * GT + i)
                with pool.Fori(5, FT // 2 - 1) as pair:
                    down_pair(g, pair)
                down_pair(g, FT // 2 - 1, last_pair=True)
            for i in range(GT):
                rstd_ln(2 * NT + (NG - 1) * GT + i)
            for i in range(GT):
                gain2((NG - 1) * GT + i)

        @block.vector
        def _(dve):
            link = chain(dve, dve_chain)
            v = nc.vector
            tt, tsc, stt = v.tensor_tensor, v.tensor_scalar, v.scalar_tensor_tensor
            v.memset(one11[:, :], 1.0)
            v.memset(neghalf[:, :, :], -0.5).then_inc(consts_ready, 1)

            def norm_stats(buf, slot, count, ready, load, load_count):
                dve.wait_ge(load, load_count)
                for b in range(2):
                    ins = v.bn_stats(stats[:, slot, 6 * b:6 * b + 6], buf[:, b * 512:(b + 1) * 512])
                link(ins)
                link(v.bn_aggr(mv[:, slot, :], stats[:, slot, :]))
                tsc(mv[:, slot, 1:2], mv[:, slot, 1:2], EPS, None, ALU.add).then_inc(ready, 1)

            def normalise(out, buf, slot, ready, count):
                dve.wait_ge(ready, count)
                return tsc(out, buf, mv[:, slot, 0:1], rstd[:, slot, :], ALU.subtract, ALU.mult)

            def x_norm(t):
                normalise(xt[:, t, :], xt[:, t, :], t % 4, rstd_ready, t + 1).then_inc(xn_ready, 1)

            for t in range(NT):
                norm_stats(xt[:, t, :], t % 4, t, var_ready, x_in[t % 3], 16 * (t // 3 + 1))
                if t >= 1:
                    x_norm(t - 1)
            x_norm(NT - 1)

            def ada_evac(b0, b1):
                link(tt(adaT[:, b0:b1, :], ps[:, 6, 2 * b0:2 * b1].rearrange("p (b w) -> p b w", w=2),
                        bc(colv[:, V_BADA + b0:V_BADA + b1].unsqueeze(2), [P, b1 - b0, 2]), ALU.add))

            dve.wait_ge(pe_adaT, 1)
            dve.wait_ge(cols_ready, 2)
            ada_evac(0, A_G1)
            tsc(ada1p[:, 0, :, :], adaT[:, A_SC1:A_SC1 + KT, :], 1.0, None, ALU.add).then_inc(ada_a, 1)
            dve.wait_ge(ada_a, 1)

            def modulate(out, bank, t, which, shift):
                w = who(t)
                for k in range(KT // 2, KT):
                    last = tsc(out[:, k, :], ps[:, bank, (k % 4) * P:(k % 4 + 1) * P], ada1p[:, which, k, w:w + 1],
                               adaT[:, shift + k, w:w + 1], ALU.mult, ALU.add)
                return last

            def lo(n):
                dve.wait_ge(whi_ready, n + 1)
                tt(wlo[:, n % 2, :], raw[:, n % RAWN, :], whi[:, n % 2, :].bitcast(F32), ALU.subtract).then_inc(wlo_dve, 1)

            def graw_evac(g):
                dve.wait_ge(pe_gate, g + 1)
                v.tensor_copy(graw[:, grp(g)], ps[0:NGATE, 7, 0:GN]).then_inc(graw_ready, 1)

            for t in range(NT):
                dve.wait_ge(pe_xT, t + 1)
                if t >= 2:
                    dve.wait_ge(h1lo_ready, t - 1)
                modulate(hm[:, t % 2, :, :], 2 * (t % 3) + 1, t, 0, A_SH1).then_inc(hm_dve, 1)
                if t == 5:
                    lo(0)
                    lo(1)
                if t >= 5 and t != 6 and t != 7:
                    graw_evac(0 if t == 5 else 1)
            graw_evac(2)

            v.memset(onesr[:, :], 1.0)
            v.memset(gi[:, :], 0.0)
            link(v.memset(gf[:, :], 0.0))
            dve.wait_ge(bg_in, 16)
            dve.wait_ge(pe_gate, NG + 1)
            gp = ps[:, 7, 0:NT * NGATE].rearrange("p (c g) -> p g c", g=NGATE)
            for typ in range(4):
                dst = (gi, gf)[typ % 2]
                d = typ // 2
                last = tt(dst[:, DIR * d:DIR * d + H * NT].rearrange("p (h c) -> p h c", c=NT),
                          gp[:, typ * H:(typ + 1) * H, :],
                          bc(bgate[:, typ * H:(typ + 1) * H].unsqueeze(2), [P, H, NT]), ALU.add)
            last.then_inc(gates_ready, 1)

            def gate_chain1():
                dve.wait_ge(pe_gT, 1)
                v.tensor_copy(li[:, :], ps[:, 7, 0:P])
                link(v.tensor_copy(fr[:, :], ps[:, 7, P:2 * P]))
                stt(lf[:, :], fr[:, :], -1.0, fr[:, :], ALU.mult, ALU.max).then_inc(f_abs, 1)

            def gate_chain2():
                dve.wait_ge(ln_ready, 1)
                link(stt(lf[:, :], fr[:, :], 0.0, Wr[:, :], ALU.min, ALU.subtract))
                fw, bw = slice(0, DIR), slice(DIR, P)
                v.tensor_tensor_scan(Bc[fw, :], onesr[fw, :], lf[fw, :], 0.0, ALU.mult, ALU.add)
                link(v.tensor_tensor_scan(Bc[bw, ::-1], onesr[bw, :], lf[bw, ::-1], 0.0, ALU.mult, ALU.add))
                link(tt(Ac[:, :], li[:, :], Bc[:, :], ALU.subtract))
                v.tensor_tensor_scan(CM[fw, :], Ac[fw, :], Ac[fw, :], -3.0e38, ALU.max, ALU.max)
                v.tensor_copy(gcol[fw, 0:1], Bc[fw, P - 1:P])
                link(v.tensor_tensor_scan(CM[bw, ::-1], Ac[bw, ::-1], Ac[bw, ::-1], -3.0e38, ALU.max, ALU.max))
                link(v.tensor_copy(gcol[bw, 0:1], Bc[bw, 0:1]))
                tt(gcol[fw, 1:2], gcol[fw, 0:1], CM[fw, P - 1:P], ALU.add)
                link(tt(gcol[bw, 1:2], gcol[bw, 0:1], CM[bw, 0:1], ALU.add))
                v.memset(mrow[:, :], 0.0).then_inc(rows_ready, 1)

            def gate_chain3():
                dve.wait_ge(pe_grow, 1)
                dve.wait_ge(m0_in, 16)
                dve.wait_ge(rows_ready, 1)
                link(v.tensor_copy(grow[:, :, :], ps[0:1, 7, 0:2 * P].rearrange("p (a b) -> p a b", b=P)))
                for d in both:
                    first = 0 if d == 0 else LT - 1
                    link(v.tensor_copy(mrow[:, rows_of(d, first)], m0row[:, d * H:(d + 1) * H]))
                for d in both:
                    for h in range(H):
                        r = row0(d, 0) + NT * h
                        if d == 0:
                            src, dst = slice(r, r + LT - 1), slice(r + 1, r + LT)
                        else:
                            src, dst = slice(r + LT - 1, r, -1), (slice(r + LT - 2, r - 1, -1) if r else slice(LT - 2, None, -1))
                        last = v.tensor_tensor_scan(mrow[:, dst], grow[:, 0, src], grow[:, 1, src],
                                                    m0row[:, d * H + h:d * H + h + 1], ALU.add, ALU.max)
                last.then_inc(mrow_ready, 1)

            def gate_chain4():
                dve.wait_ge(pe_mcol, 1)
                link(v.tensor_copy(gcol[:, 2:3], ps[:, 7, 0:1]))
                tsc(nM[:, :], CM[:, :], gcol[:, 2:3], -1.0, ALU.max, ALU.mult)
                link(tt(gcol[:, 6:7], gcol[:, 0:1], gcol[:, 2:3], ALU.add))
                link(tt(gcol[:, 3:4], gcol[:, 6:7], gcol[:, 1:2], ALU.max))
                tt(gcol[:, 4:5], gcol[:, 6:7], gcol[:, 3:4], ALU.subtract)
                link(tt(gcol[:, 5:6], gcol[:, 0:1], gcol[:, 3:4], ALU.subtract))
                tt(enm[:, :], nM[:, :], Bc[:, :], ALU.subtract).then_inc(exps_in, 1)

            def gate_chain5():
                dve.wait_ge(pe_tok, 1)
                v.tensor_copy(tok[:, 0, :], ps[:, 7, 0:P])
                tsc(tok[:, 1, :], ps[:, 7, P:2 * P], QK_SCALE, None, ALU.mult)
                v.tensor_copy(tok[:, 2, :], ps[:, 7, 2 * P:3 * P])
                v.tensor_copy(decb[:, :], ps[:, 7, 3 * P:4 * P]).then_inc(tok_ready, 1)
                dve.wait_ge(pe_ada, N_ADA1)
                v.memset(v1[:, :, :, P:P + 1], 1.0).then_inc(v_ready, 1)

            def v_evac(h, part):
                j = 3 * h + part
                dve.wait_ge(pe_v, j + 1)
                c0, c1 = 4 * part, min(4 * part + 4, NT)
                v.tensor_copy(v1[:, c0:c1, h, 0:P], ps[:, 7, 0:(c1 - c0) * P].rearrange("p (c n) -> p c n", n=P)
                              ).then_inc(v_ready, 1)

            def conv(j):
                tile = 2 * H + j
                dve.wait_ge(tile_out, tile + 1)
                if j < H:
                    dve.wait_ge(pe_v, 3 * (j + 1))
                else:
                    dve.wait_ge(pe_pool, 3 * (j - H + 1))
                src, dst = work[:, tile % 2, :], qk[:, j, :]
                w = [colv[:, V_CONV + KT * a + j:V_CONV + KT * a + j + 1] for a in range(3)]
                link(tsc(dst, src, w[1], None, ALU.mult))
                for a in (0, 2):
                    for t0, t1 in ((0, LAT), (LAT, T)):
                        o, i_ = (slice(t0 + 1, t1), slice(t0, t1 - 1)) if a == 0 else (slice(t0, t1 - 1), slice(t0 + 1, t1))
                        last = stt(dst[:, o], src[:, i_], w[a], dst[:, o], ALU.mult, ALU.add)
                    if a == 0:
                        link(last)
                last.then_inc(conv_done, 1)

            def arow_evac(j):
                dve.wait_ge(pe_ada, N_ADA1 + 2 * (j - N_ADA1) + 2)
                v.tensor_copy(arow[:, j % 2, :], ps[0:2, 6, ADA_AT:ADA_AT + AC]).then_inc(arow_ready, 1)

            for n in range(2 * NPROJ):
                if n >= 2 and n % 2 == 0:
                    arow_evac(N_ADA1 + n // 2 - 1)
                job = JOBS.get(n - 1, ("",))
                if job[0] == "v":
                    v_evac(job[1], job[2])
                if n == 9:
                    gate_chain5()
                if n == 5:
                    gate_chain3()
                if n == 7:
                    gate_chain4()
                if n + 2 < U_C:
                    lo(n + 2)
                if n == 2:
                    gate_chain1()
                if n == 3:
                    gate_chain2()
                if n % 2 == 0 and n // 2 > 2 * H:
                    conv(n // 2 - 1 - 2 * H)
            arow_evac(N_ADA - 1)
            conv(2 * H - 1)
            dve.wait_ge(pe_adaT, 2)
            ada_evac(A_G1, 6 * KT)
            tsc(ada1p[:, 1, :, :], adaT[:, A_SC2:A_SC2 + KT, :], 1.0, None, ALU.add).then_inc(ada_b, 1)

            dve.wait_ge(tok_ready, 1)

            def head_cols(table, d, ck, shape):
                return bc(table[:, rows_of(d, ck)].unsqueeze(2), shape)

            def d_add(s, d):
                ck = scan_chunks(s)[d]
                D = Dm[:, s % 2, d, :, :]
                dve.wait_ge(dm_in[s % 2][d], 16 * (s // 2 + 1))
                tt(D, D, head_cols(tok[:, 0, :], d, ck, [P, H, P]), ALU.add).then_inc(d_added[d], 1)

            def p_make(s, d):
                dve.wait_ge(pe_s[d], s + 1)
                dve.wait_ge(d_sel[d], s + 1)
                D = Dm[:, s % 2, d, :, :].rearrange("p h n -> p (h n)")
                stt(D, ps[:, 3 + d, :], QK_SCALE, D, ALU.mult, ALU.mult).then_inc(p_ready[d], 1)

            def kw_make(s, d):
                ck = scan_chunks(s)[d]
                dve.wait_ge(pe_kt[d], s + 1)
                if s >= 1:
                    dve.wait_ge(pe_u[d], 2 * s if s < LT else 2 * s - 2)
                tt(kw[:, d, :, :], ps[:, 5, :].rearrange("p (h n) -> p h n", h=H),
                   head_cols(tok[:, 1, :], d, ck, [P, H, P]), ALU.mult).then_inc(kw_ready[d], 1)

            seen = set()

            def num_evac(s, d):
                ck = scan_chunks(s)[d]
                for pair in range(2):
                    dve.wait_ge(pe_num[d], 2 * s + pair + 1)
                    acc2 = ps[:, 6 + pair, 0:2 * (P + 1)].rearrange("p (h n) -> p h n", h=2)
                    r = rows_of(d, ck)
                    em = tok[:, 2, r][:, 2 * pair:2 * pair + 2].unsqueeze(2)
                    link(stt(rden[:, :, :], acc2[:, :, P:P + 1], -1.0, em, ALU.mult, ALU.max))
                    link(tt(rden[:, :, :], rden[:, :, :], acc2[:, :, P:P + 1], ALU.max))
                    link(v.reciprocal(rden[:, :, :], rden[:, :, :]))
                    out = hacc[:, ck, 2 * pair:2 * pair + 2, :]
                    rb = bc(rden[:, :, :], [P, 2, P])
                    if (ck, pair) not in seen:
                        seen.add((ck, pair))
                        ins = tt(out, acc2[:, :, 0:P], rb, ALU.mult)
                        ins.then_inc(num_used[d], 1)
                        dve.wait_ge(num_used[d], 2 * s + pair + 1)
                    else:
                        ins = tt(tmph[:, :, :], acc2[:, :, 0:P], rb, ALU.mult)
                        ins.then_inc(num_used[d], 1)
                        dve.wait_ge(num_used[d], 2 * s + pair + 1)
                        link(tt(out, out, tmph[:, :, :], ALU.add))

            def u_add(s, d):
                ck = scan_chunks(s)[d]
                for pair in range(2):
                    dve.wait_ge(pe_u[d], (2 * s if s < LT else 2 * s - 2) + pair + 1)
                    for hh in range(2):
                        h = 2 * pair + hh
                        add = ps[:, 6 + pair, hh * (P + 1):(hh + 1) * (P + 1)]
                        r = row0(d, ck) + NT * h
                        if s < LT:
                            last = stt(Cs[:, d, h, :], Cs[:, d, h, :], decb[:, r:r + 1], add, ALU.mult, ALU.add)
                        else:
                            last = v.tensor_copy(Cs[:, d, h, :], add)
                    last.then_inc(u_used[d], 1)

            fin = [0, 0]

            def h_stats():
                ck = final[fin[0]][1]
                b = fin[0] % 2
                for h in range(H):
                    last = v.bn_stats(sth[:, b, h, :], hacc[:, ck, h, :])
                link(last)
                for h in range(H):
                    last = v.bn_aggr(mvh[:, b, h, :], sth[:, b, h, :])
                link(last)
                tsc(mvh[:, b, :, 1:2], mvh[:, b, :, 1:2], EPS, None, ALU.add).then_inc(hvar_ready, 1)
                fin[0] += 1

            def h_norm():
                ck = final[fin[1]][1]
                b = fin[1] % 2
                dve.wait_ge(hrstd_ready, fin[1] + 1)
                hc = hacc[:, ck, :, :]
                link(tt(hc, hc, bc(mvh[:, b, :, 0:1], [P, H, P]), ALU.subtract))
                tt(hc, hc, bc(rsh[:, b, :, :], [P, H, P]), ALU.mult).then_inc(hn_ready, 1)
                fin[1] += 1

            d_add(0, 0)
            d_add(0, 1)
            dve.wait_ge(cs_in, 64)
            for s in range(NSTEP):
                p_make(s, 0)
                p_make(s, 1)
                kw_make(s, 0)
                if 1 <= s < LT:
                    u_add(s - 1, 1)
                if s + 1 < NSTEP:
                    d_add(s + 1, 0)
                kw_make(s, 1)
                num_evac(s, 0)
                if s + 1 < NSTEP:
                    d_add(s + 1, 1)
                for _ in [ck for at, ck in final if at == s - 1]:
                    h_norm()
                num_evac(s, 1)
                if s < LT - 1 or s == LT:
                    u_add(s, 0)
                for _ in [ck for at, ck in final if at == s]:
                    h_stats()
            u_add(LT, 1)
            h_norm()

            dve.wait_ge(sig_ready, 1)
            dve.wait_ge(hT_used, NT)
            for g in range(NG):
                for h in range(H):
                    last = stt(qk[:, h, grp(g)], qk[:, h, grp(g)], colv[:, V_HN + h:V_HN + h + 1], work[:, h, grp(g)],
                               ALU.mult, ALU.mult)
                last.then_inc(ml_ready, 1)

            nst = [0]

            def residual(t, buf, tmp, rows, out_sem, out_count, used, before):
                g, i = t // GT, t % GT
                dve.wait_ge(y_in[t % 4], 16 * (t // 4 + 1 + before * times(t % 4)))
                for half in range(2):
                    dve.wait_ge(out_sem, out_count(g, i, half))
                    cols = slice(half * 512, (half + 1) * 512)
                    tt(tmp[:, cols], ps[:, out_bank(g, 2 * i + half), :], rows[:, who(t), cols], ALU.mult).then_inc(used, 1)
                dve.wait_ge(used, 2 * (t + 1))
                link(stt(buf[:, t % 4, :], buf[:, t % 4, :], ALPHA, tmp[:, :], ALU.mult, ALU.add))

            def ln_stats(buf):
                slot = nst[0] % 4
                for b in range(2):
                    ins = v.bn_stats(stats[:, slot, 6 * b:6 * b + 6], buf[:, b * 512:(b + 1) * 512])
                link(ins)
                link(v.bn_aggr(mv[:, slot, :], stats[:, slot, :]))
                tsc(mv[:, slot, 1:2], mv[:, slot, 1:2], EPS, None, ALU.add).then_inc(lvar, 1)
                nst[0] += 1

            def ln_norm(out, buf, j):
                return normalise(out, buf, j % 4, lrstd, j + 1)

            dve.wait_ge(ada_b, 1)
            dve.wait_ge(grows_ready, 1)
            for g in range(NG):
                j0 = nst[0]
                tiles = range(g * GT, (g + 1) * GT)
                if g >= 1:
                    dve.wait_ge(pe_yT, g * GT)
                for t in tiles:
                    residual(t, yt, tb, grows, pe_unit, lambda g, i, half: U_OUT + (g + 1) * KT * 2, out_used, 0)
                for t in tiles:
                    ln_stats(yt[:, t % 4, :])
                for i, t in enumerate(tiles):
                    ln_norm(yt[:, t % 4, :], yt[:, t % 4, :], j0 + i).then_inc(lnorm, 1)
                for i, t in enumerate(tiles):
                    dve.wait_ge(x1_ready, t + 1)
                    ln_stats(yt[:, t % 4, :])
                    if t >= 1:
                        dve.wait_ge(pe_yT, t)
                    ln_norm(tb[:, :], yt[:, t % 4, :], j0 + GT + i).then_inc(tb_ready, 1)
                    dve.wait_ge(pe_yT, t + 1)
                    if t >= 1:
                        dve.wait_ge(h2lo_ready, t)
                    modulate(hm2, out_bank(min(g + 1, NG - 1), 2 * GT) + 1, t, 1, A_SH2).then_inc(hm2_dve, 1)

            lat3 = [x[:, 0:LAT].rearrange("p (r w) -> p r w", w=GRID_W) for x in (gs, acc)]

            others = [(dy, dx) for dx in (-1, 0, 1) for dy in (-1, 0, 1) if (dy, dx) != (0, 0)]
            n_conv = len(others) + 3

            def shifted(n, d):
                return slice(max(0, -d), n - max(0, d)), slice(max(0, d), n - max(0, -d))

            def up_tile(i):
                def step(ins, m):
                    ins.then_inc(conv_step, 1)
                    dve.wait_ge(conv_step, n_conv * i + m)

                dve.wait_ge(g_out, i + 1)
                v.tensor_copy(taps[:, 0:NTAP], dwc[:, :].rearrange("p (t f) -> p t f", f=FT)[:, :, bass.ds(i, 1)])
                step(v.tensor_copy(taps[:, NTAP:NTAP + 1], colv[:, bass.ds(i + V_BDW, 1)]), 1)
                step(tsc(acc[:, :], gs[:, :], taps[:, 4:5], None, ALU.mult), 2)
                for m, (dy, dx) in enumerate(others):
                    tap = 3 * (dy + 1) + dx + 1
                    (ro, ri), (co, ci) = shifted(GRID_H, dy), shifted(GRID_W, dx)
                    step(stt(lat3[1][:, ro, co], lat3[0][:, ri, ci], taps[:, tap:tap + 1], lat3[1][:, ro, co],
                             ALU.mult, ALU.add), 3 + m)
                for dx in (-1, 1):
                    co, ci = shifted(CTX, dx)
                    ins = stt(acc[:, LAT:T][:, co], gs[:, LAT:T][:, ci], taps[:, 4 + dx:5 + dx], acc[:, LAT:T][:, co],
                              ALU.mult, ALU.add)
                    if dx < 0:
                        step(ins, n_conv)
                    else:
                        ins.then_inc(conv_ready, 1)
                dve.wait_ge(gelu_ready, i + 1)
                dve.wait_ge(pe_unit, 4 * i + (U_UP + 4))
                tt(u[:, bass.ds(i, 1), :].rearrange("p a (g n) -> p (a g) n", g=NG),
                   acc[:, :].rearrange("p (g n) -> p g n", g=NG), ps[:, 3:6, 0:GN], ALU.mult).then_inc(u_ready, 1)

            up_tile(0)
            for b in range(4):
                dve.wait_ge(y_out[b], 16 * times(b))
            with dve.Fori(1, FT) as i:
                up_tile(i)

            dve.wait_ge(ln2_in, 32)
            dve.wait_ge(grows2_ready, 2)
            for g in range(NG):
                j0 = nst[0]
                tiles = range(g * GT, (g + 1) * GT)
                for t in tiles:
                    residual(t, zt, zb, grows2, pe_unit, lambda g, i, half: U_DOWN + (g + 1) * 2 * FT - 1 + half, down_used, 1)
                for t in tiles:
                    ln_stats(zt[:, t % 4, :])
                for i, t in enumerate(tiles):
                    ln_norm(zt[:, t % 4, :], zt[:, t % 4, :], j0 + i).then_inc(lnorm, 1)


_INS = ["x_prompt", "x_sample", "c", "state_C", "state_n", "state_m", "c_ctx", "w_ada", "b_ada", "w_in", "b_gates",
        "w_qk_conv", "hn_g", "w_pool", "pool_scale", "w_out", "ln1_g", "ln1_b", "w_up", "w_dw", "b_dw", "w_down",
        "ln2_g", "ln2_b"]
_OUTS = [(1, CTX, DM), (1, LAT, DM), (1, 1, 2, H, P, P), (1, 1, 2, H, P), (1, 1, 2, H)]


def inverse_counts():
    def line(length, w):
        t = np.arange(length)
        return 1.0 / (np.minimum(t + w // 2, length) - np.maximum(t - w // 2, 0))
    return np.stack([np.concatenate([line(GRID_H, w), line(GRID_W, w), line(CTX, w)]) for w in WINDOWS]).astype(np.float32)


def kernel(**inputs):
    import concourse.bacc as _bacc
    from concourse.bass_utils import run_bass_kernel_spmd as _run

    nc = _bacc.Bacc("TRN2", target_bir_lowering=False, num_devices=1)
    arrays, args = {}, []
    for name in _INS + ["inv_count"]:
        a = inverse_counts() if name == "inv_count" else np.ascontiguousarray(inputs[name])
        arrays[f"in_{name}"] = a
        args.append(nc.dram_tensor(f"in_{name}", a.shape, F32, kind="ExternalInput").ap())
    for i, shape in enumerate(_OUTS):
        args.append(nc.dram_tensor(f"out_{i}", shape, F32, kind="ExternalOutput").ap())
    args.append(nc.dram_tensor("scan_rows", (2, P, P), F32).ap())
    args.append(nc.dram_tensor("pool_out", (P, H, T), F32).ap())
    args.append(nc.dram_tensor("x1_rows", (NT, P, DM), F32).ap())
    layer(nc, *args)
    r = _run(nc, [arrays], core_ids=[0])
    return tuple(r.results[0][f"out_{i}"] for i in range(len(_OUTS)))
```

```python
import concourse.bass as bass
from concourse import mybir
import numpy as np
from contextlib import ExitStack

F32 = mybir.dt.float32
F32R = mybir.dt.float32r
ALU = mybir.AluOpType
ACT = mybir.ActivationFunctionType

P = 128
DM = 1024
KT = DM // P
LAT, CTX = 1024, 128
T = LAT + CTX
NT = T // P
LT = NT - 1
GN = 384
NG = T // GN
GT = GN // P
H = 4
GRID_W, GRID_H = 64, 16
WINDOWS = (2, 4, 8, 16)
FF = 2816
FT = FF // P
NGATE = 16
ALPHA = 2.0 ** 0.25
EPS = 1e-5
QK_SCALE = float(P) ** -0.5

UC = 512
RAWN = 4
NPROJ = 16
N_ACT_TAP = 6
U_LO = 28
U_C = 2 * NPROJ
U_OUT = U_C + 2 * H
U_UP = U_OUT + NG * KT * 2
U_DOWN = U_UP + FT * 4
U_END = U_DOWN + NG * FT * 2

V_C, V_CC, V_BADA, V_HN, V_PS, V_CONV, V_BDW, NV = 0, 8, 16, 64, 68, 72, 96, 118
A_SH1, A_SC1, A_G1, A_SH2, A_SC2, A_G2 = (KT * i for i in range(6))
AC = 256
N_ADA1 = 2 * DM // AC
N_ADA = 6 * DM // AC
ADA1_RING = 6
ADA_AT = 2 * 6 * KT
NTAP = 9
DIR = 64
PADW = GRID_W + 16
PADC = CTX + 16


def proj_col(tile):
    kind, j = tile // H, tile % H
    return (0, 3 * H, H, 2 * H, 4 * H)[kind] * P + j * P


JOBS = {1: ("gT",), 4: ("grow",), 6: ("mcol",), 8: ("tok",)}
for _n in range(12):
    JOBS[10 + _n] = ("v", _n // 3, _n % 3)
for _n in range(10):
    JOBS[22 + _n] = ("pool", _n // 3, _n % 3)
LATE_JOBS = (("pool", 3, 1), ("pool", 3, 2))


def layer(nc, x_prompt, x_sample, c, state_C, state_n, state_m, c_ctx, w_ada, b_ada, w_in, b_gates,
          w_qk_conv, hn_g, w_pool, pool_scale, w_out, ln1_g, ln1_b, w_up, w_dw, b_dw, w_down,
          ln2_g, ln2_b, inv_count, y_prompt, y_sample, new_C, new_n, new_m, scan_rows, gate_rows, pool_out, x1_rows):
    with ExitStack() as stack, nc.allow_non_contiguous_dma(reason="normaliser column of the state, stabiliser rows"):
        def sem(name):
            return stack.enter_context(nc.semaphore(name))

        top = [(nc.sbuf_base + 63) // 64 * 64]

        def place(name, shape, at=None, dt=F32):
            size = 4 * int(np.prod(shape[1:]))
            if at is None:
                at = top[0]
                top[0] = (at + size + 31) // 32 * 32
            return nc.alloc_sbuf_tensor_at(name, shape, dt, offset=(at + 31) // 32 * 32)

        raw = place("raw", [P, RAWN, UC])
        whi = place("whi", [P, 2, UC], dt=F32R)
        wlo = place("wlo", [P, 2, UC], dt=F32R)
        ident = place("ident", [P, P])
        colv = place("colv", [P, NV])
        dwc = place("dwc", [P, NTAP * FT])
        adaT = place("adaT", [P, 6 * KT, 2])
        ada1p = place("ada1p", [P, 2, KT, 2])
        neghalf = place("neghalf", [P, H, 1])
        one11 = place("one11", [P, 1])
        pick = place("pick", [P, 2, 2])
        stats = place("stats", [P, 4, 12])
        mv = place("mv", [P, 4, 2])
        rstd = place("rstd", [P, 4, 1])
        taps = place("taps", [P, NTAP + 1])
        wgr = place("wgr", [P, KT, NGATE])
        wghi = place("wghi", [P, KT, NGATE], dt=F32R)
        wglo = place("wglo", [P, KT, NGATE], dt=F32R)
        M0 = top[0]
        big = 4 * KT * T

        h1hi = place("h1hi", [P, KT, T], M0, F32R)
        h1lo = place("h1lo", [P, KT, T], M0 + big, F32R)
        qk_at = M0 + 2 * big
        qk = place("qk", [P, 2 * H, T], qk_at)
        v1_at = qk_at + big
        v1 = place("v1", [P, NT, H, P + 1], v1_at)
        hacc_at = (v1_at + 4 * NT * H * (P + 1) + 31) // 32 * 32
        hacc = place("hacc", [P, NT, H, P], hacc_at)
        poolA = place("poolA", [P, 2048], hacc_at)
        poolB = place("poolB", [P, 2048], hacc_at + 8192)
        adaw1 = place("adaw1", [P, ADA1_RING, KT, AC], qk_at)
        xt_at = qk_at + 4 * ADA1_RING * KT * AC
        xt = place("xt", [P, NT, DM], xt_at)
        work_at = hacc_at + 4 * NT * H * P
        work = place("work", [P, 4, T], work_at)
        past_xt = xt_at + 4 * NT * DM
        assert work_at < past_xt
        rowsv = place("rowsv", [P, P], past_xt)
        rowsd = place("rowsd", [P, 2, P], past_xt + 512)
        bgate = place("bgate", [P, NGATE], past_xt + 1536)
        graw = place("graw", [NGATE, T], past_xt + 1600)
        assert past_xt + 1600 + 4 * T <= work_at + 16 * T
        wpl = place("wpl", [P, H, P], work_at + 4 * 2 * T)
        aacc = place("aacc", [P, 2, AC], work_at + 16 * T - 8 * AC)
        po = place("po", [P, GN], work_at + 4 * 2 * T + 4 * H * P)
        pohi = place("pohi", [P, GN], work_at + 4 * 2 * T + 4 * (H * P + GN), F32R)
        polo = place("polo", [P, GN], work_at + 4 * 2 * T + 4 * (H * P + 2 * GN), F32R)
        top[0] = work_at + 16 * T
        cs_at = top[0]
        Cs = place("Cs", [P, 2, H, P + 1])
        tok = place("tok", [P, 3, P])
        decb = place("decb", [P, P])
        gcol = place("gcol", [P, 8])
        grow_at = top[0]
        grow = place("grow", [1, 2, P])
        growT = place("growT", [2 * KT, 2, P], grow_at)
        mrow = place("mrow", [1, P])
        m0row = place("m0row", [1, 2 * H])
        tmp_at = top[0]
        Dm = place("Dm", [P, 2, 2, H, P])
        Qa = place("Qa", [P, 2, H, P])
        kw = place("kw", [P, 2, H, P])
        mvh = place("mvh", [P, 2, H, 2])
        sth = place("sth", [P, 2, H, 6])
        rsh = place("rsh", [P, 2, H, 1])
        rden = place("rden", [P, 2, 1])
        tmph = place("tmph", [P, 2, P])
        assert top[0] <= nc.sbuf_usable_end, (top[0], nc.sbuf_usable_end)
        top[0] = tmp_at
        hm = place("hm", [P, 2, KT, P], tmp_at)
        adaw = place("adaw", [P, 2, KT // 2, AC])
        arow = place("arow", [2, 2, AC])
        gi, gf, li, fr, lf, Bc, Ac, CM, nM, ai, enm, Wr = [place(n, [P, P]) for n in
            "gi gf li fr lf Bc Ac CM nM ai enm Wr".split()]
        invt = place("invt", [P, 4, GRID_H + GRID_W + CTX], cs_at)
        onesr = place("onesr", [P, P])
        assert top[0] <= nc.sbuf_usable_end, (top[0], nc.sbuf_usable_end)
        mixhi = place("mixhi", [P, KT, T], M0, F32R)
        mixlo = place("mixlo", [P, KT, T], M0 + big, F32R)
        top[0] = M0 + 2 * big
        yt = place("yt", [P, 4, DM])
        tb = place("tb", [P, DM])
        lnrows = place("lnrows", [P, 2, DM])
        h2hi = place("h2hi", [P, KT, T], dt=F32R)
        h2lo = place("h2lo", [P, KT, T], dt=F32R)
        gs = place("gs", [P, T])
        grows = place("grows", [P, 2, DM], top[0] - 4 * T)
        acc = place("acc", [P, T])
        hm2_at = top[0]
        hm2 = place("hm2", [P, KT, P])
        top[0] = hm2_at
        ushi = place("ushi", [P, 2, GN], dt=F32R)
        uslo = place("uslo", [P, 2, GN], dt=F32R)
        assert top[0] <= nc.sbuf_usable_end, (top[0], nc.sbuf_usable_end)
        u = place("u", [P, FT, T], M0)
        top[0] = M0 + 4 * FT * T
        zt = place("zt", [P, 4, DM])
        zb = place("zb", [P, DM])
        grows2 = place("grows2", [P, 2, DM])
        lnrows2 = place("lnrows2", [P, 2, DM])
        assert top[0] <= hm2_at

        ps = stack.enter_context(nc.psum_tensor("ps", [P, 8, 512], F32))

        raw_in = [sem(f"raw_in{b}") for b in range(RAWN)]
        whi_ready, wlo_dve, wlo_pool, pe_unit = sem("whi_ready"), sem("wlo_dve"), sem("wlo_pool"), sem("pe_unit")
        dve_chain, act_chain, pool_chain = sem("dve_chain"), sem("act_chain"), sem("pool_chain")
        rows_in, rowsd_in, bg_in, wg_in = sem("rows_in"), sem("rowsd_in"), sem("bg_in"), sem("wg_in")
        inv_in, m0_in, wpl_in, cs_in = sem("inv_in"), sem("m0_in"), sem("wpl_in"), sem("cs_in")
        x_in = [sem(f"x_in{b}") for b in range(3)]
        ada1_in = [sem(f"ada1_in{b}") for b in range(ADA1_RING)]
        ada_used = sem("ada_used")
        arow_ready, pe_adaT, graw_ready = sem("arow_ready"), sem("pe_adaT"), sem("graw_ready")
        ada_in = [sem(f"ada_in{b}") for b in range(2)]
        ones_ready = sem("ones_ready")
        ident_ready, consts_ready, rows_silu = sem("ident_ready"), sem("consts_ready"), sem("rows_silu")
        pe_rows, cols_ready, pe_ada, ada_a, ada_b = sem("pe_rows"), sem("cols_ready"), sem("pe_ada"), sem("ada_a"), sem("ada_b")
        var_ready, rstd_ready, xn_ready, pe_xT = sem("var_ready"), sem("rstd_ready"), sem("xn_ready"), sem("pe_xT")
        hm_act, hm_dve, h1hi_ready, h1lo_ready = sem("hm_act"), sem("hm_dve"), sem("h1hi_ready"), sem("h1lo_ready")
        wghi_ready, wglo_ready, pe_gate, gates_ready = sem("wghi_ready"), sem("wglo_ready"), sem("pe_gate"), sem("gates_ready")
        pe_gT, f_abs, ln_ready, rows_ready, pe_grow = sem("pe_gT"), sem("f_abs"), sem("ln_ready"), sem("rows_ready"), sem("pe_grow")
        mrow_ready, pe_mcol, exps_in, exps_ready, pe_tok, tok_ready = (sem("mrow_ready"), sem("pe_mcol"), sem("exps_in"),
            sem("exps_ready"), sem("pe_tok"), sem("tok_ready"))
        rows_out = sem("rows_out")
        tile_out, conv_done, silu_done = sem("tile_out"), sem("conv_done"), sem("silu_done")
        pool_y, pe_v, v_ready, pe_pool, po_ready = sem("pool_y"), sem("pe_v"), sem("v_ready"), sem("pe_pool"), sem("po_ready")
        pohi_ready, polo_ready, pohi_out, polo_out = sem("pohi_ready"), sem("polo_ready"), sem("pohi_out"), sem("polo_out")
        both = range(2)
        dm_in = [[sem(f"dm_in{p}{d}") for d in both] for p in both]
        qa_in = [sem(f"qa_in{d}") for d in both]
        d_added, d_exp, d_sel, qa_ready = ([sem(f"{n}{d}") for d in both] for n in ("d_added", "d_exp", "d_sel", "qa_ready"))
        pe_s, p_ready, pe_kt, kw_ready = ([sem(f"{n}{d}") for d in both] for n in ("pe_s", "p_ready", "pe_kt", "kw_ready"))
        pe_num, num_used, pe_u, u_used = ([sem(f"{n}{d}") for d in both] for n in ("pe_num", "num_used", "pe_u", "u_used"))
        hvar_ready, hrstd_ready, hn_ready, pe_hT, hT_used = (sem("hvar_ready"), sem("hrstd_ready"), sem("hn_ready"),
            sem("pe_hT"), sem("hT_used"))
        state_out = sem("state_out")
        pool_back, sig_ready, ml_ready = sem("pool_back"), sem("sig_ready"), sem("ml_ready")
        mixhi_ready, mixlo_ready = sem("mixhi_ready"), sem("mixlo_ready")
        pe_grows, growT_ready, gate_out, grows_in, ln_in = (sem("pe_grows"), sem("growT_ready"), sem("gate_out"),
            sem("grows_in"), sem("ln_in"))
        y_in = [sem(f"y_in{b}") for b in range(4)]
        pe_out, out_used, t_added = sem("pe_out"), sem("out_used"), sem("t_added")
        g_mult = sem("g_mult")
        lvar, lrstd, lnorm, x1_ready = sem("lvar"), sem("lrstd"), sem("lnorm"), sem("x1_ready")
        y_out = [sem(f"y_out{b}") for b in range(4)]
        tb_ready, pe_yT, hm2_act, h2hi_ready, h2lo_ready = (sem("tb_ready"), sem("pe_yT"), sem("hm2_act"),
            sem("h2hi_ready"), sem("h2lo_ready"))
        g_out, conv_step, conv_ready, gelu_ready, u_ready = (sem("g_out"), sem("conv_step"), sem("conv_ready"),
            sem("gelu_ready"), sem("u_ready"))
        ushi_ready, uslo_ready = sem("ushi_ready"), sem("uslo_ready")
        ln2_in = sem("ln2_in")
        down_used, z_ready = sem("down_used"), sem("z_ready")

        def chain(engine, semaphore):
            count = [0]

            def link(ins):
                count[0] += 1
                ins.then_inc(semaphore, 1)
                engine.wait_ge(semaphore, count[0])
            return link

        def x_rows(x_s, x_p, t):
            return x_s[0, t * P:(t + 1) * P, :] if t < LT else x_p[0, :, :]

        def who(t):
            return int(t >= LT)

        def bc(ap, shape):
            return ap.to_broadcast(shape)

        def times(b):
            return len(range(b, NT, 4))

        def grp(g):
            return slice(g * GN, (g + 1) * GN)

        def chunk(t):
            return slice(t * P, (t + 1) * P)

        def scan_chunks(s):
            return (s, LT - 1 - s) if s < LT else (LT, LT)

        def row0(d, ck):
            return DIR * d + ck

        def rows_of(d, ck):
            return slice(row0(d, ck), row0(d, ck) + NT * (H - 1) + 1, NT)

        NSTEP = NT
        N_GM = NT - 2

        def out_bank(g, i):
            return (2 * GT * g + i) % 8

        def down_bank(g, i):
            return (2 * GT * g + i + 6) % 8

        def lo_ready(n):
            pool_mix, pool_up, dve_down = U_OUT - U_LO, (U_OUT + U_UP) // 2 - U_LO, (U_UP - U_OUT) // 2 + U_LO
            if n < U_LO:
                return wlo_dve, n + 1
            if n < U_OUT:
                return wlo_pool, n - U_LO + 1
            if n < U_UP:
                return (wlo_pool, pool_mix + (n - U_OUT) // 2 + 1) if n % 2 else (wlo_dve, U_LO + (n - U_OUT) // 2 + 1)
            if n < U_DOWN:
                return wlo_pool, pool_up + n - U_UP + 1
            return (wlo_pool, pool_up + U_DOWN - U_UP + (n - U_DOWN) // 2 + 1) if n % 2 else (
                wlo_dve, dve_down + (n - U_DOWN) // 2 + 1)

        def wait_lo(eng, n):
            eng.wait_ge(*lo_ready(n))

        def wait_raw_free(eng, n):
            if n >= RAWN:
                wait_lo(eng, n - RAWN)

        def h_bank(ck):
            return 5 if ck < LT else 7

        def raw_wait(eng, n):
            eng.wait_ge(raw_in[n % RAWN], 16 * (n // RAWN + 1))

        final = [(s, ck) for s in range(LT // 2, LT) for ck in scan_chunks(s)] + [(LT, LT)]

        block = stack.enter_context(nc.Block())

        @block.sync
        def _(sp):
            for src, r in ((c.rearrange("a (r f) -> (a r) f", f=P), V_C),
                           (c_ctx.rearrange("(r f) -> r f", f=P), V_CC),
                           (b_ada.rearrange("a (r f) -> (a r) f", f=P), V_BADA),
                           (hn_g.rearrange("a (r f) -> (a r) f", f=P), V_HN),
                           (pool_scale.rearrange("a (r f) -> (a r) f", f=P), V_PS),
                           (w_qk_conv.rearrange("a t (r f) -> (a t r) f", f=P), V_CONV),
                           (b_dw.rearrange("a (r f) -> (a r) f", f=P), V_BDW)):
                sp.dma_start(rowsv[r:r + src.shape[0], :], src).then_inc(rows_in, 16)
            ada_v = w_ada[0].rearrange("(k p) n -> p k n", p=P)

            def load_ada1(i):
                if i >= ADA1_RING:
                    sp.wait_ge(pe_ada, i - ADA1_RING + 1)
                sp.dma_start(adaw1[:, i % ADA1_RING, :, :], ada_v[:, :, i * AC:(i + 1) * AC]
                             ).then_inc(ada1_in[i % ADA1_RING], 16)

            def load_x0(t):
                if t >= 3:
                    sp.wait_ge(x_in[t % 3], 16 * (t // 3))
                sp.dma_start(xt[:, t, :], x_rows(x_sample, x_prompt, t)).then_inc(x_in[t % 3], 16)

            load_ada1(0)
            load_ada1(1)
            load_x0(0)
            load_ada1(2)
            load_x0(1)
            load_ada1(3)
            load_x0(2)
            load_ada1(4)
            load_ada1(5)
            taps_v = w_dw[0].rearrange("a b (f e) -> (a b f) e", e=P)
            for j in range(2):
                sp.dma_start(rowsd[0:NTAP * FT // 2, j, :],
                             taps_v[j * NTAP * FT // 2:(j + 1) * NTAP * FT // 2, :]).then_inc(rowsd_in, 16)
            sp.dma_start(wgr[:, :, :], w_in[0, :, 5 * H * P:5 * H * P + NGATE].rearrange("(k p) n -> p k n", p=P)
                         ).then_inc(wg_in, 16)
            load_ada1(6)
            load_x0(3)
            load_ada1(7)
            for t in range(4, NT):
                load_x0(t)
            sp.dma_start(bgate[:, :], b_gates[0].partition_broadcast(P)).then_inc(bg_in, 16)

            proj_v = w_in[0].rearrange("(k p) n -> p k n", p=P)

            def load_proj(n):
                wait_raw_free(sp, n)
                col = proj_col(n // 2)
                sp.dma_start(raw[:, n % RAWN, :].rearrange("p (k n) -> p k n", k=KT // 2),
                             proj_v[:, (n % 2) * KT // 2:(n % 2 + 1) * KT // 2, col:col + P]
                             ).then_inc(raw_in[n % RAWN], 16)

            for n in range(RAWN):
                load_proj(n)
            sp.dma_start(m0row[:, :], state_m[0].rearrange("a d h -> a (d h)")).then_inc(m0_in, 16)
            sp.dma_start(invt[:, :, :], inv_count.partition_broadcast(P)).then_inc(inv_in, 16)
            sp.wait_ge(pe_xT, NT)
            sp.wait_ge(h1lo_ready, NT)
            sp.dma_start(wpl[:, :, :], w_pool[0].rearrange("g c d -> c g d")).then_inc(wpl_in, 16)
            po_n = 0

            def spill_pool():
                nonlocal po_n
                g, r = po_n // 3, po_n % 3
                sp.wait_ge(pohi_ready, po_n + 1)
                sp.dma_start(pool_out[0, :, g, grp(r)], pohi[:, :].bitcast(F32)).then_inc(pohi_out, 16)
                sp.wait_ge(polo_ready, po_n + 1)
                sp.dma_start(pool_out[1, :, g, grp(r)], polo[:, :].bitcast(F32)).then_inc(polo_out, 16)
                po_n += 1

            for n in range(2 * NPROJ):
                if n >= 2:
                    sp.wait_ge(ada_used, n - 1)
                blk = N_ADA1 + n // 2
                sp.dma_start(adaw[:, n % 2, :, :], ada_v[:, (n % 2) * KT // 2:(n % 2 + 1) * KT // 2, blk * AC:(blk + 1) * AC]
                             ).then_inc(ada_in[n % 2], 16)
                if n + RAWN < U_OUT:
                    load_proj(n + RAWN)
                if n == 12:
                    sp.wait_ge(exps_ready, 1)
                    sp.dma_start(scan_rows[0], nM[:, :]).then_inc(rows_out, 16)
                    sp.dma_start(scan_rows[1], ai[:, :]).then_inc(rows_out, 16)
                    for d in both:
                        sp.dma_start(new_m[0, 0, d].rearrange("(h a) -> h a", a=1),
                                     gcol[rows_of(d, LT), 3:4]).then_inc(state_out, 16)
                if n >= 23:
                    spill_pool()

            def scan_load(s):
                for d in both:
                    if s >= 2:
                        sp.wait_ge(pe_num[d], 2 * (s - 1))
                    sp.dma_start(Dm[:, s % 2, d, :, :], scan_rows[0, rows_of(d, scan_chunks(s)[d]), :].partition_broadcast(P)
                                 ).then_inc(dm_in[s % 2][d], 16)
                if s < LT:
                    for d in both:
                        if s >= 1:
                            sp.wait_ge(pe_num[d], 2 * s)
                        sp.dma_start(Qa[:, d, :, :], scan_rows[1, rows_of(d, scan_chunks(s)[d]), :].partition_broadcast(P)
                                     ).then_inc(qa_in[d], 16)

            while po_n < 11:
                spill_pool()
            sp.wait_ge(rows_out, 32)
            sp.wait_ge(pe_adaT, 2)
            sp.wait_ge(tok_ready, 1)
            sp.wait_ge(pool_y, 4)
            scan_load(0)
            for d in both:
                sp.dma_start(Cs[:, d, :, 0:P], state_C[0, 0, d].rearrange("h k v -> k h v")).then_inc(cs_in, 16)
                sp.dma_start(Cs[:, d, :, P:P + 1],
                             state_n[0, 0, d].rearrange("h (k a) -> k h a", a=1)).then_inc(cs_in, 16)
            while po_n < 12:
                spill_pool()
            sp.wait_ge(growT_ready, 1)
            sp.dma_start(gate_rows.rearrange("g r f -> r g f"), growT[:, :, :]).then_inc(gate_out, 16)
            for s in range(NSTEP):
                if s + 1 < NSTEP:
                    scan_load(s + 1)
                if 2 * NPROJ + s + RAWN < U_OUT:
                    load_proj(2 * NPROJ + s + RAWN)

            def load_out(n):
                wait_raw_free(sp, n)
                j = n - U_OUT
                k, half = (j // 2) % KT, j % 2
                sp.dma_start(raw[:, n % RAWN, :], w_out[0, k * P:(k + 1) * P, half * UC:(half + 1) * UC]
                             ).then_inc(raw_in[n % RAWN], 16)

            for n in range(U_OUT, U_OUT + RAWN):
                load_out(n)
            for d in both:
                sp.wait_ge(u_used[d], 2 * NSTEP - 2)
                sp.dma_start(new_C[0, 0, d].rearrange("h k v -> k h v"), Cs[:, d, :, 0:P]).then_inc(state_out, 16)
                sp.dma_start(new_n[0, 0, d].rearrange("h (k a) -> k h a", a=1), Cs[:, d, :, P:P + 1]).then_inc(state_out, 16)

            def load_x(t):
                if t >= 4:
                    sp.wait_ge(y_out[t % 4], 16 * (t // 4))
                    sp.wait_ge(tb_ready, t - 3)
                sp.dma_start(yt[:, t % 4, :], x_rows(x_sample, x_prompt, t)).then_inc(y_in[t % 4], 16)

            def store_x1(t):
                sp.wait_ge(x1_ready, t + 1)
                sp.dma_start(x1_rows[t], yt[:, t % 4, :]).then_inc(y_out[t % 4], 16)

            def load_gate_rows(dst, g, done):
                for w in both:
                    sp.dma_start(dst[:, w, :].rearrange("p (k f) -> p k f", f=P), gate_rows[g, w::2, :].partition_broadcast(P)
                                 ).then_inc(done, 16)

            for n in range(U_OUT + RAWN, U_UP):
                g, r = divmod(n - U_OUT, 2 * KT)
                if n in (U_OUT + 5, U_OUT + 6):
                    for d in both:
                        sp.wait_ge(pe_kt[d], NSTEP)
                        sp.wait_ge(pe_s[d], NSTEP)
                    row, vector = ((0, ln1_g), (1, ln1_b))[n - U_OUT - 5]
                    sp.dma_start(lnrows[:, row, :], vector[0].partition_broadcast(P)).then_inc(ln_in, 16)
                if n == U_OUT + 8:
                    for d in both:
                        sp.wait_ge(pe_u[d], 2 * NSTEP - 2)
                    sp.wait_ge(gate_out, 16)
                    load_gate_rows(grows, 0, grows_in)
                if n == U_OUT + 12:
                    sp.wait_ge(mixlo_ready, NG)
                if U_OUT + 12 <= n < U_OUT + 12 + GT:
                    load_x(n - U_OUT - 12)
                if g >= 1:
                    if r == 2:
                        load_x(GT * g)
                    if r == 12:
                        store_x1(GT * g - 3)
                    if r == 14:
                        load_x(GT * g + 1)
                        store_x1(GT * g - 2)
                if g >= 2 and r == 0:
                    load_x(GT * g - 1)
                    store_x1(GT * (g - 1) - 1)
                load_out(n)
            load_x(NT - 1)
            store_x1(GT * (NG - 1) - 1)
            up_v = w_up[0].rearrange("(k p) n -> p k n", p=P)

            def load_up(i, col):
                for q in range(4):
                    if i is None:
                        wait_raw_free(sp, U_UP + q)
                    else:
                        free, count = lo_ready(U_UP + q)
                        sp.wait_ge(free, 4 * i + (count - RAWN))
                    unit = up_v[:, (q % 2) * KT // 2:(q % 2 + 1) * KT // 2, bass.ds(col + (FF if q < 2 else 0), P)]
                    sp.dma_start(raw[:, q, :].rearrange("p (k n) -> p k n", k=KT // 2), unit).then_inc(raw_in[q], 16)

            load_up(None, 0)
            for t in range(NT - GT, NT):
                store_x1(t)
            with sp.Fori(0, FT - 1) as before:
                load_up(before + 1, P * before + P)

            first_pair = 0

            def load_down(g, pair):
                rows2 = [bass.ds(pair * 2 * P + b * P, P) for b in both]
                for q in range(4):
                    unit = w_down[0, rows2[q // 2], (q % 2) * UC:(q % 2 + 1) * UC]
                    if g == 0 and pair is first_pair:
                        wait_raw_free(sp, U_DOWN + q)
                    else:
                        free, count = lo_ready(U_DOWN + g * 2 * FT + q)
                        sp.wait_ge(free, 2 * pair + (count - RAWN // 2))
                    sp.dma_start(raw[:, q, :], unit).then_inc(raw_in[q], 16)

            load_down(0, 0)
            sp.wait_ge(pe_unit, U_DOWN)
            load_gate_rows(grows2, 1, grows_in)
            sp.dma_start(lnrows2[:, 0, :], ln2_g[0].partition_broadcast(P)).then_inc(ln2_in, 16)
            sp.dma_start(lnrows2[:, 1, :], ln2_b[0].partition_broadcast(P)).then_inc(ln2_in, 16)
            for b in range(4):
                sp.wait_ge(y_out[b], 16 * times(b))
            for t in range(GT):
                sp.dma_start(zt[:, t % 4, :], x1_rows[t]).then_inc(y_in[t % 4], 16)

            def store_y(t):
                sp.wait_ge(z_ready, t + 1)
                sp.dma_start(x_rows(y_sample, y_prompt, t), zt[:, t % 4, :]).then_inc(y_out[t % 4], 16)

            for g in range(NG):
                if g > 0:
                    load_down(g, 0)
                with sp.Fori(1, 9) as pair:
                    load_down(g, pair)
                if g > 0:
                    for i in range(GT - 1):
                        store_y((g - 1) * GT + i)
                    for i in range(GT):
                        t = g * GT + i
                        if t >= 4:
                            sp.wait_ge(y_out[t % 4], 16 * (t // 4 + times(t % 4)))
                        sp.dma_start(zt[:, t % 4, :], x1_rows[t]).then_inc(y_in[t % 4], 16)
                with sp.Fori(9, FT // 2) as pair:
                    load_down(g, pair)
                if g > 0:
                    store_y(g * GT - 1)
            for i in range(GT):
                store_y((NG - 1) * GT + i)
            for b in range(4):
                sp.wait_ge(y_out[b], 16 * 2 * times(b))
            sp.wait_ge(state_out, 96)

        @block.tensor
        def _(pe):
            mm = nc.tensor.matmul
            pe.wait_ge(ident_ready, 2)
            pe.wait_ge(rows_silu, 1)
            nc.tensor.transpose(ps[:, 7, 0:NV], rowsv[0:NV, :], ident[0:NV, 0:NV]).then_inc(pe_rows, 1)

            def x_transposes(t):
                pe.wait_ge(xn_ready, t + 1)
                if t >= 3:
                    pe.wait_ge(hm_act, t - 2)
                    pe.wait_ge(hm_dve, t - 2)
                for k in range(KT):
                    last = nc.tensor.transpose(ps[:, 2 * (t % 3) + k // 4, (k % 4) * P:(k % 4 + 1) * P],
                                               xt[:, t, k * P:(k + 1) * P], ident[:, :])
                last.then_inc(pe_xT, 1)

            n_half = NTAP * FT // 2
            def ada_mm(k, w):
                return mm(ps[0:2, 6, ADA_AT:ADA_AT + AC], colv[:, V_C + k:V_CC + k + 1:V_CC - V_C], w,
                          start=(k == 0), stop=(k == KT - 1))

            def ada_transposes(j):
                pe.wait_ge(arow_ready, j + 1)
                for b in range(AC // P):
                    blk = j * AC // P + b
                    last = nc.tensor.transpose(ps[:, 6, 2 * blk:2 * blk + 2], arow[:, j % 2, b * P:(b + 1) * P],
                                               ident[0:2, 0:2])
                return last

            pe.wait_ge(cols_ready, 1)
            for i in range(N_ADA1):
                if i >= 1:
                    ada_transposes(i - 1)
                if i in (3, 5, 7):
                    x_transposes((i - 3) // 2)
                if i == 6:
                    pe.wait_ge(rowsd_in, 32)
                    for j in range(2):
                        last = nc.tensor.transpose(ps[:, 7, P * (j + 1):P * (j + 1) + n_half], rowsd[0:n_half, j, :],
                                                   ident[0:n_half, 0:n_half])
                    last.then_inc(pe_rows, 1)
                pe.wait_ge(ada1_in[i % ADA1_RING], 16 * (i // ADA1_RING + 1))
                for k in range(KT):
                    last = ada_mm(k, adaw1[:, i % ADA1_RING, k, :])
                last.then_inc(pe_ada, 1)
            ada_transposes(N_ADA1 - 1).then_inc(pe_adaT, 1)

            def ada_rows(m):
                pe.wait_ge(ada_used, 2 * m + 2)
                for w in both:
                    last = mm(ps[0:2, 6, ADA_AT:ADA_AT + AC], pick[:, w, :], aacc[:, w, :], start=(w == 0), stop=(w == 1))
                last.then_inc(pe_ada, 1)

            def gate_group(g):
                pe.wait_ge(h1lo_ready, GT * (g + 1))
                if g >= 1:
                    pe.wait_ge(graw_ready, g)
                for k in range(KT):
                    for a, b in ((wghi, h1hi), (wghi, h1lo), (wglo, h1hi)):
                        last = mm(ps[0:NGATE, 7, 0:GN], a[:, k, :], b[:, k, grp(g)],
                                  start=(k == 0 and a is wghi and b is h1hi), stop=(k == KT - 1 and a is wglo))
                last.then_inc(pe_gate, 1)

            for t in range(3, 6):
                x_transposes(t)
            pe.wait_ge(wglo_ready, 1)
            pe.wait_ge(cols_ready, 2)
            gate_group(0)
            for t in range(6, NT):
                x_transposes(t)
            gate_group(1)

            def gate_transposes():
                pe.wait_ge(graw_ready, NG)
                for t in range(NT):
                    last = nc.tensor.transpose(ps[:, 7, t * NGATE:(t + 1) * NGATE], graw[:, chunk(t)],
                                               ident[0:NGATE, 0:NGATE])
                last.then_inc(pe_gate, 1)

            def proj_group(n, bank, g):
                for k in range(KT // 2):
                    kk = (n % 2) * KT // 2 + k
                    for a, b in ((whi, h1hi), (whi, h1lo), (wlo, h1hi)):
                        last = mm(ps[:, bank, 0:GN], a[:, n % 2, k * P:(k + 1) * P], b[:, kk, grp(g)],
                                  start=(kk == 0 and a is whi and b is h1hi), stop=(kk == KT - 1 and a is wlo))
                return last

            jobs_done = {"v": 0, "pool": 0}

            def misc_job(job):
                kind = job[0]
                if kind == "gT":
                    pe.wait_ge(gates_ready, 1)
                    nc.tensor.transpose(ps[:, 7, 0:P], gi[:, :], ident[:, :])
                    nc.tensor.transpose(ps[:, 7, P:2 * P], gf[:, :], ident[:, :]).then_inc(pe_gT, 1)
                elif kind == "grow":
                    pe.wait_ge(rows_ready, 1)
                    for j in range(2):
                        last = mm(ps[0:1, 7, j * P:(j + 1) * P], gcol[:, j:j + 1], ident[:, :], start=True, stop=True)
                    last.then_inc(pe_grow, 1)
                elif kind == "mcol":
                    pe.wait_ge(mrow_ready, 1)
                    mm(ps[:, 7, 0:1], mrow[0:1, :], one11[0:1, :], start=True, stop=True).then_inc(pe_mcol, 1)
                elif kind == "tok":
                    pe.wait_ge(exps_ready, 1)
                    for j, src in enumerate((Ac, Wr, enm)):
                        nc.tensor.transpose(ps[:, 7, j * P:(j + 1) * P], src[:, :], ident[:, :])
                    mm(ps[:, 7, 3 * P:4 * P], bc(gcol[:, 4:5], [P, P]), ident[:, :], start=True, stop=True).then_inc(pe_tok, 1)
                elif kind == "v":
                    _, h, part = job
                    pe.wait_ge(tok_ready, 1)
                    pe.wait_ge(tile_out, H + h + 1)
                    if jobs_done["v"]:
                        pe.wait_ge(v_ready, jobs_done["v"] + 1)
                    for ck in range(4 * part, min(4 * part + 4, NT)):
                        last = nc.tensor.transpose(ps[:, 7, (ck % 4) * P:(ck % 4 + 1) * P], qk[:, h, chunk(ck)], ident[:, :])
                    last.then_inc(pe_v, 1)
                    jobs_done["v"] += 1
                elif kind == "pool":
                    _, g, part = job
                    pe.wait_ge(v_ready, 13)
                    pe.wait_ge(wpl_in, 16)
                    pe.wait_ge(pool_y, g + 1)
                    if jobs_done["pool"]:
                        pe.wait_ge(po_ready, jobs_done["pool"])
                    mm(ps[:, 7, 0:GN], wpl[:, g, :], qk[:, H + g, grp(part)], start=True, stop=True).then_inc(pe_pool, 1)
                    jobs_done["pool"] += 1

            for n in range(2 * NPROJ):
                tile, bank = n // 2, 3 * ((n // 2) % 2)
                wait_lo(pe, n)
                if n == 2:
                    pe.wait_ge(hm_act, NT)
                    pe.wait_ge(hm_dve, NT)
                if n % 2 == 0 and tile >= 2:
                    pe.wait_ge(tile_out, tile - 1)
                for g in range(NG):
                    if n == 0 and g == 0:
                        pe.wait_ge(hm_act, 7)
                        pe.wait_ge(hm_dve, 7)
                    if n == 0 and g == 2:
                        gate_group(2)
                        pe.wait_ge(hm_act, 8)
                        pe.wait_ge(hm_dve, 8)
                    last = proj_group(n, bank + g, g)
                last.then_inc(pe_unit, 1)
                if n and n % 2 == 0:
                    if n >= 4:
                        ada_transposes(N_ADA1 + n // 2 - 2)
                    ada_rows(n // 2 - 1)
                if n == 0:
                    gate_transposes()
                if n in JOBS:
                    misc_job(JOBS[n])

            def o_unit(n, g):
                if g == 0:
                    wait_lo(pe, n)
                    if n % 2 == 0:
                        pe.wait_ge(tile_out, NPROJ - 1 if n == U_C else NPROJ + (n - U_C) // 2)
                last = proj_group(n, g, g)
                if g == NG - 1:
                    last.then_inc(pe_unit, 1)

            misc_job(LATE_JOBS[0])
            ada_transposes(N_ADA - 2)
            o_unit(U_C, 0)
            ada_rows(N_ADA - N_ADA1 - 1)
            misc_job(LATE_JOBS[1])
            o_unit(U_C, 1)
            ada_transposes(N_ADA - 1).then_inc(pe_adaT, 1)
            pe.wait_ge(ada_b, 1)
            for j, a in enumerate((A_G1, A_G2)):
                last = nc.tensor.transpose(ps[0:2 * KT, 6, j * P:(j + 1) * P],
                                           adaT[:, a:a + KT, :].rearrange("p k w -> p (k w)"), ident[:, :])
            last.then_inc(pe_grows, 1)
            o_unit(U_C, 2)

            def scores(s, d):
                ck = scan_chunks(s)[d]
                if s == 0:
                    pe.wait_ge(silu_done, 2 * H)
                    pe.wait_ge(tile_out, NPROJ)
                else:
                    pe.wait_ge(p_ready[d], s)
                for h in range(H):
                    last = mm(ps[:, 3 + d, h * P:(h + 1) * P], qk[:, H + h, chunk(ck)], qk[:, h, chunk(ck)],
                              start=True, stop=True)
                last.then_inc(pe_s[d], 1)

            def k_transposes(s, d):
                ck = scan_chunks(s)[d]
                if d == 1:
                    pe.wait_ge(kw_ready[0], s + 1)
                elif s >= 1:
                    pe.wait_ge(kw_ready[1], s)
                    if hT[0]:
                        pe.wait_ge(hT_used, hT[0])
                for h in range(H):
                    last = nc.tensor.transpose(ps[:, 5, h * P:(h + 1) * P], qk[:, H + h, chunk(ck)], ident[:, :])
                last.then_inc(pe_kt[d], 1)

            def numerators(s, d):
                ck = scan_chunks(s)[d]
                pe.wait_ge(p_ready[d], s + 1)
                if s < LT:
                    pe.wait_ge(qa_ready[d], s + 1)
                    if s == 0:
                        pe.wait_ge(cs_in, 64)
                        pe.wait_ge(growT_ready, 1)
                        pe.wait_ge(po_ready, 12)
                    elif s >= 1:
                        pe.wait_ge(u_used[d], 2 * s)
                if d == 1:
                    pe.wait_ge(num_used[0], 2 * s + 2)
                elif s >= 1:
                    pe.wait_ge(u_used[1] if s < LT else num_used[1], 2 * s)
                for pair in range(2):
                    for hh in range(2):
                        h = 2 * pair + hh
                        out = ps[:, 6 + pair, hh * (P + 1):(hh + 1) * (P + 1)]
                        last = mm(out, Dm[:, s % 2, d, h, :], v1[:, ck, h, :], start=True, stop=(s == LT))
                        if s < LT:
                            last = mm(out, Qa[:, d, h, :], Cs[:, d, h, :], start=False, stop=True)
                    last.then_inc(pe_num[d], 1)

            def updates(s, d):
                ck = scan_chunks(s)[d]
                pe.wait_ge(kw_ready[d], s + 1)
                if d == 0:
                    pe.wait_ge(num_used[1], 2 * s + 2)
                else:
                    pe.wait_ge(u_used[0], 2 * s + 2 if s < LT else 2 * s)
                for pair in range(2):
                    for hh in range(2):
                        h = 2 * pair + hh
                        last = mm(ps[:, 6 + pair, hh * (P + 1):(hh + 1) * (P + 1)], kw[:, d, h, :], v1[:, ck, h, :],
                                  start=True, stop=True)
                    last.then_inc(pe_u[d], 1)

            hT = [0]

            def h_transposes(ck):
                pe.wait_ge(hn_ready, hT[0] + 1)
                if ck < LT:
                    if hT[0]:
                        pe.wait_ge(hT_used, hT[0])
                    pe.wait_ge(kw_ready[1], final[hT[0]][0] + 2)
                else:
                    pe.wait_ge(u_used[1], 2 * NSTEP - 2)
                for h in range(H):
                    last = nc.tensor.transpose(ps[:, h_bank(ck), h * P:(h + 1) * P], hacc[:, ck, h, :], ident[:, :])
                last.then_inc(pe_hT, 1)
                hT[0] += 1

            for s in range(NSTEP):
                n = U_C + s + 1

                def slot(g):
                    if n < U_OUT:
                        o_unit(n, g)

                scores(s, 0)
                scores(s, 1)
                k_transposes(s, 0)
                if 1 <= s < LT:
                    updates(s - 1, 1)
                slot(0)
                k_transposes(s, 1)
                numerators(s, 0)
                slot(1)
                done = [ck for at, ck in final if at == s - 1]
                numerators(s, 1)
                for ck in done[:1]:
                    h_transposes(ck)
                slot(2)
                if s != LT - 1:
                    updates(s, 0)
                for ck in done[1:]:
                    h_transposes(ck)
            updates(LT, 1)
            def y_transposes(t, g):
                bank = out_bank(g, 2 * GT)
                pe.wait_ge(tb_ready, t + 1)
                if t < NT - GT:
                    pe.wait_ge(out_used, 2 * GT * (t // GT + 1))
                if t >= 1:
                    pe.wait_ge(hm2_act, t)
                for k in range(KT):
                    last = nc.tensor.transpose(ps[:, bank + k // 4, (k % 4) * P:(k % 4 + 1) * P],
                                               tb[:, k * P:(k + 1) * P], ident[:, :])
                last.then_inc(pe_yT, 1)

            pe.wait_ge(tile_out, NPROJ + H)
            pe.wait_ge(p_ready[1], NSTEP)
            pe.wait_ge(kw_ready[1], NSTEP)
            pe.wait_ge(hT_used, LT)
            pe.wait_ge(pool_back, 32)
            for g in range(NG):
                for k in range(KT):
                    for half in range(2):
                        n = U_OUT + (g * KT + k) * 2 + half
                        wait_lo(pe, n)
                        if k == H and half == 0:
                            pe.wait_ge(mixhi_ready, g + 1)
                            pe.wait_ge(mixlo_ready, g + 1)
                        for i in range(GT):
                            bank = out_bank(g, 2 * i + half)
                            if k == 0:
                                before = 2 * GT * g + 2 * i + half - 8
                                if before >= 0:
                                    pe.wait_ge(out_used, before + 1)
                                if g == 1 and i == 0:
                                    pe.wait_ge(hT_used, NT)
                                if g == 2 and i == 0:
                                    pe.wait_ge(hm2_act, GT)
                            for a, b in ((mixhi, whi), (mixhi, wlo), (mixlo, whi)):
                                last = mm(ps[:, bank, :], a[:, k, chunk(g * GT + i)], b[:, n % 2, :],
                                          start=(k == 0 and a is mixhi and b is whi), stop=(k == KT - 1 and a is mixlo))
                        last.then_inc(pe_unit, 1)
                    if g == 0 and k == 1:
                        h_transposes(LT)
                    if g >= 1 and k >= 5:
                        y_transposes((g - 1) * GT + k - 5, g)
            def first_gate(q, g):
                for k in range(KT // 2):
                    kk = q * KT // 2 + k
                    for a, b in ((whi, h2hi), (whi, h2lo), (wlo, h2hi)):
                        last = mm(ps[:, 4 + g, 0:GN], a[:, q, k * P:(k + 1) * P], b[:, kk, grp(g)],
                                  start=(kk == 0 and a is whi and b is h2hi), stop=(kk == KT - 1 and a is wlo))
                return last

            wait_lo(pe, U_UP)
            wait_lo(pe, U_UP + 1)
            for g in range(NG - 1):
                pe.wait_ge(h2lo_ready, GT * (g + 1))
                pe.wait_ge(out_used, 2 * (NT - GT) + g + 1)
                for q in range(2):
                    first_gate(q, g)
            for i in range(GT):
                y_transposes((NG - 1) * GT + i, NG - 1)
            pe.wait_ge(h2lo_ready, NT)
            for q in range(2):
                first_gate(q, NG - 1).then_inc(pe_unit, 1)

            def up_tile(i, first=False):
                for q in range(2 if first else 0, 4):
                    ready, count = lo_ready(U_UP + q)
                    pe.wait_ge(ready, 4 * i + count)
                    if q == 0:
                        pe.wait_ge(g_out, i)
                    if q == 2:
                        if first:
                            pe.wait_ge(g_out, 1)
                            pe.wait_ge(hm2_act, NT)
                        else:
                            pe.wait_ge(u_ready, i)
                    for g in range(NG):
                        for k in range(KT // 2):
                            kk = (q % 2) * KT // 2 + k
                            for a, b in ((whi, h2hi), (whi, h2lo), (wlo, h2hi)):
                                last = mm(ps[:, 3 * (q // 2) + g, 0:GN], a[:, q % 2, k * P:(k + 1) * P], b[:, kk, grp(g)],
                                          start=(kk == 0 and a is whi and b is h2hi), stop=(kk == KT - 1 and a is wlo))
                    last.then_inc(pe_unit, 1)

            pe.wait_ge(out_used, 2 * NT)
            up_tile(0, first=True)
            with pe.Fori(1, FT) as i:
                up_tile(i)

            def down_pair(g, pair, first=False, final_pair=False):
                for q in range(4):
                    ready, count = lo_ready(U_DOWN + g * 2 * FT + q)
                    pe.wait_ge(ready, 2 * pair + count)
                    if q % 2 == 0:
                        pe.wait_ge(uslo_ready, 2 * pair + (g * FT + q // 2 + 1))
                    for i in range(GT):
                        bank = down_bank(g, 2 * i + q % 2)
                        if first and q < 2:
                            if g >= 1:
                                before = 2 * GT * g + 2 * i + q % 2 - 8
                                if before >= 0:
                                    pe.wait_ge(down_used, before + 1)
                            elif bank == 3:
                                pe.wait_ge(u_ready, FT)
                            elif bank == 0:
                                pe.wait_ge(g_out, FT)
                        for a, b in ((ushi, whi), (ushi, wlo), (uslo, whi)):
                            last = mm(ps[:, bank, :], a[:, q // 2, i * P:(i + 1) * P], b[:, q % 2, :],
                                      start=(first and q < 2 and a is ushi and b is whi),
                                      stop=(final_pair and q >= 2 and a is uslo))
                    last.then_inc(pe_unit, 1)

            for g in range(NG):
                down_pair(g, 0, first=True)
                with pe.Fori(1, FT // 2 - 1) as pair:
                    down_pair(g, pair)
                down_pair(g, FT // 2 - 1, final_pair=True)

        @block.scalar
        def _(act):
            link = chain(act, act_chain)
            fn = nc.scalar.activation

            def hi(n):
                raw_wait(act, n)
                if n >= 2:
                    act.wait_ge(pe_unit, n - 1)
                fn(whi[:, n % 2, :], raw[:, n % RAWN, :], ACT.Copy).then_inc(whi_ready, 1)

            act.wait_ge(rows_in, 7 * 16)
            fn(rowsv[0:V_BADA, :], rowsv[0:V_BADA, :], ACT.Silu).then_inc(rows_silu, 1)
            act.wait_ge(pe_rows, 1)
            fn(colv[:, :], ps[:, 7, 0:NV], ACT.Copy).then_inc(cols_ready, 1)
            half = NTAP * FT // 2
            for i in range(N_ADA1):
                if i == 6:
                    act.wait_ge(pe_rows, 2)
                    fn(dwc[:, :].rearrange("p (j n) -> p j n", j=2),
                       ps[:, 7, P:3 * P].rearrange("p (j n) -> p j n", j=2)[:, :, 0:half], ACT.Copy).then_inc(cols_ready, 1)
                    act.wait_ge(wg_in, 16)
                    fn(wghi[:, :, :], wgr[:, :, :], ACT.Copy).then_inc(wghi_ready, 1)
                act.wait_ge(pe_ada, i + 1)
                fn(arow[:, i % 2, :], ps[0:2, 6, ADA_AT:ADA_AT + AC], ACT.Copy).then_inc(arow_ready, 1)
            act.wait_ge(ada_a, 1)
            for t in range(NT):
                act.wait_ge(pe_xT, t + 1)
                if t >= 2:
                    act.wait_ge(h1lo_ready, t - 1)
                w = who(t)
                for k in range(KT // 2):
                    last = fn(hm[:, t % 2, k, :], ps[:, 2 * (t % 3), k * P:(k + 1) * P], ACT.Identity,
                              scale=ada1p[:, 0, k, w:w + 1], bias=adaT[:, A_SH1 + k, w:w + 1])
                last.then_inc(hm_act, 1)
                act.wait_ge(hm_act, t + 1)
                act.wait_ge(hm_dve, t + 1)
                fn(h1hi[:, :, chunk(t)], hm[:, t % 2, :, :], ACT.Copy).then_inc(h1hi_ready, 1)
                if t == 4:
                    hi(0)
                    hi(1)

            def po_evac(j):
                act.wait_ge(pe_pool, j + 1)
                if j >= 1:
                    act.wait_ge(polo_ready, j)
                    act.wait_ge(pohi_out, 16 * j)
                g = j // 3
                fn(po[:, :], ps[:, 7, 0:GN], ACT.Copy, scale=colv[:, V_PS + g:V_PS + g + 1]).then_inc(po_ready, 1)
                act.wait_ge(po_ready, j + 1)
                fn(pohi[:, :], po[:, :], ACT.Copy).then_inc(pohi_ready, 1)

            def silu(j):
                act.wait_ge(conv_done, j + 1)
                fn(qk[:, j, :], qk[:, j, :], ACT.Silu).then_inc(silu_done, 1)

            act.wait_ge(h1lo_ready, NT)
            for n in range(2 * NPROJ):
                job = JOBS.get(n - 1, ("",))
                if job[0] == "pool":
                    po_evac(3 * job[1] + job[2])
                hi(n + 2)
                if n % 2:
                    tile = n // 2
                    act.wait_ge(pe_unit, n + 1)
                    if tile < H:
                        dst = qk[:, H + tile, :]
                    elif tile < 2 * H:
                        dst = qk[:, tile - H, :]
                    else:
                        dst = work[:, tile % 2, :]
                        if tile >= 2 * H + 2:
                            act.wait_ge(conv_done, tile - 2 * H - 1)
                    b0 = 3 * (tile % 2)
                    j = tile - 2 * H
                    if 0 <= j < N_ACT_TAP:
                        if j < H:
                            act.wait_ge(pe_v, 3 * (j + 1))
                        else:
                            act.wait_ge(pe_pool, 3 * (j - H + 1))
                        fn(qk[:, j, :].rearrange("p (g n) -> p g n", g=NG), ps[:, b0:b0 + 3, 0:GN], ACT.Copy,
                           scale=colv[:, V_CONV + KT + j:V_CONV + KT + j + 1])
                    fn(dst.rearrange("p (g n) -> p g n", g=NG), ps[:, b0:b0 + 3, 0:GN], ACT.Copy).then_inc(tile_out, 1)
                    if 2 * H < tile < NPROJ - 1:
                        silu(tile - 2 * H - 1)
                if n == 2:
                    act.wait_ge(f_abs, 1)
                    link(fn(Wr[:, :], lf[:, :], ACT.Exp, scale=-1.0))
                    fn(Wr[:, :], Wr[:, :], ACT.Ln, bias=1.0).then_inc(ln_ready, 1)
                if n == 7:
                    act.wait_ge(exps_in, 1)
                    fn(ai[:, :], nM[:, :], ACT.Exp, bias=gcol[:, 2:3])
                    fn(enm[:, :], enm[:, :], ACT.Exp)
                    fn(gcol[:, 4:5], gcol[:, 4:5], ACT.Exp)
                    fn(Wr[:, :], Ac[:, :], ACT.Exp, bias=gcol[:, 5:6]).then_inc(exps_ready, 1)
            po_evac(9)
            po_evac(10)
            silu(2 * H - 2)
            po_evac(11)
            silu(2 * H - 1)
            act.wait_ge(pe_grows, 1)
            fn(growT[:, :, :], ps[0:2 * KT, 6, 0:2 * P].rearrange("p (g f) -> p g f", g=2), ACT.Copy).then_inc(growT_ready, 1)

            def d_exps(s, d):
                act.wait_ge(d_added[d], s + 1)
                D = Dm[:, s % 2, d, :, :]
                fn(D, D, ACT.Exp).then_inc(d_exp[d], 1)

            fin = [0]

            def h_evac():
                ck = final[fin[0]][1]
                act.wait_ge(pe_hT, fin[0] + 1)
                fn(qk[:, 0:H, chunk(ck)], ps[:, h_bank(ck), :].rearrange("p (h n) -> p h n", h=H), ACT.Copy
                   ).then_inc(hT_used, 1)
                fin[0] += 1

            d_exps(0, 0)
            d_exps(0, 1)
            for s in range(NSTEP):
                n = U_C + s
                if n < U_OUT:
                    if s % 2:
                        act.wait_ge(pe_unit, n + 1)
                        fn(work[:, s // 2, :].rearrange("p (g n) -> p g n", g=NG), ps[:, 0:3, 0:GN], ACT.Copy).then_inc(tile_out, 1)
                    hi(n + 2)
                if s + 1 < NSTEP:
                    d_exps(s + 1, 0)
                    d_exps(s + 1, 1)
                for _ in [ck for at, ck in final if at == s - 1]:
                    h_evac()
            act.wait_ge(tile_out, NPROJ + H)
            for j in range(H):
                last = fn(work[:, j, :], work[:, j, :], ACT.Sigmoid)
            last.then_inc(sig_ready, 1)

            def mix_hi(g):
                act.wait_ge(ml_ready, g + 1)
                fn(mixhi[:, H:2 * H, grp(g)], qk[:, 0:H, grp(g)], ACT.Copy).then_inc(mixhi_ready, 1)

            def modulate2(t, bank):
                act.wait_ge(pe_yT, t + 1)
                if t >= 1:
                    act.wait_ge(h2lo_ready, t)
                w = who(t)
                for k in range(KT):
                    last = fn(hm2[:, k, :], ps[:, bank + k // 4, (k % 4) * P:(k % 4 + 1) * P], ACT.Identity,
                              scale=ada1p[:, 1, k, w:w + 1], bias=adaT[:, A_SH2 + k, w:w + 1])
                last.then_inc(hm2_act, 1)
                act.wait_ge(hm2_act, t + 1)
                fn(h2hi[:, :, chunk(t)], hm2[:, :, :], ACT.Copy).then_inc(h2hi_ready, 1)

            for g in range(NG):
                for k in range(KT):
                    for half in range(2):
                        hi(U_OUT + (g * KT + k) * 2 + half + 2)
                        r = 2 * k + half
                        if g == 0:
                            if r == 2:
                                mix_hi(0)
                            if r == 4:
                                h_evac()
                                mix_hi(1)
                            if r == 7:
                                mix_hi(2)
                    if g >= 1 and k >= 5:
                        modulate2((g - 1) * GT + k - 5, out_bank(g, 2 * GT))
            for i in range(GT):
                modulate2((NG - 1) * GT + i, out_bank(NG - 1, 2 * GT))

            def up_tile(i, first=False, last_tile=False):
                for q in range(4):
                    m = q + 2
                    act.wait_ge(raw_in[m % 4], 16 * i + 16 * (U_UP // 4 + 1 + m // 4))
                    act.wait_ge(pe_unit, 4 * i + (U_UP + q + 1))
                    fn(whi[:, m % 2, :], raw[:, m % 4, :], ACT.Copy).then_inc(whi_ready, 1)
                    if q == 1:
                        g0 = 4 if first else 0
                        if not first:
                            act.wait_ge(conv_ready, i)
                        fn(gs[:, :].rearrange("p (g n) -> p g n", g=NG), ps[:, g0:g0 + 3, 0:GN], ACT.Copy).then_inc(g_out, 1)
                if not last_tile:
                    gelu(i)

            def gelu(i):
                act.wait_ge(conv_ready, 1 * i + 1)
                fn(acc[:, :], acc[:, :], ACT.Gelu_apprx_tanh, bias=taps[:, NTAP:NTAP + 1]).then_inc(gelu_ready, 1)

            up_tile(0, first=True)
            with act.Fori(1, FT - 1) as i:
                up_tile(i)
            up_tile(FT - 1, last_tile=True)

            def down_pair(g, pair, last_pair=False):
                base = U_DOWN + g * 2 * FT
                for q in range(4):
                    if not (last_pair and g == NG - 1 and q >= 2):
                        m = q + 2
                        act.wait_ge(raw_in[m % 4], 16 * pair + 16 * (base // 4 + 1 + m // 4))
                        act.wait_ge(pe_unit, 4 * pair + (base + q + 1))
                        fn(whi[:, m % 2, :], raw[:, m % 4, :], ACT.Copy).then_inc(whi_ready, 1)
                    if q % 2 == 1:
                        if last_pair:
                            if g < NG - 1:
                                fn(ushi[:, q // 2, :], u[:, q // 2, grp(g + 1)], ACT.Copy).then_inc(ushi_ready, 1)
                        else:
                            fn(ushi[:, q // 2, :], u[:, bass.ds(2 * pair + (2 + q // 2), 1), grp(g)], ACT.Copy
                               ).then_inc(ushi_ready, 1)

            for b in range(2):
                fn(ushi[:, b, :], u[:, b, grp(0)], ACT.Copy).then_inc(ushi_ready, 1)
            gelu(FT - 1)
            act.wait_ge(u_ready, FT)
            for g in range(NG):
                down_pair(g, 0)
                with act.Fori(1, FT // 2 - 1) as pair:
                    down_pair(g, pair)
                down_pair(g, FT // 2 - 1, last_pair=True)

        @block.gpsimd
        def _(pool):
            link = chain(pool, pool_chain)
            nc.gpsimd.memset(ident[:, :], 0.0).then_inc(ident_ready, 1)
            pool.wait_ge(ident_ready, 1)
            nc.gpsimd.affine_select(out=ident[:, :], in_=ident[:, :], compare_op=ALU.not_equal, fill=1.0, base=0,
                                    pattern=[[-1, P]], channel_multiplier=1).then_inc(ident_ready, 1)

            def sub_hi(out, full, hi_part):
                return nc.gpsimd.tensor_tensor(out, full, hi_part.bitcast(F32), ALU.subtract)

            pool.wait_ge(consts_ready, 1)
            for t in range(NT):
                pool.wait_ge(var_ready, t + 1)
                nc.gpsimd.tensor_tensor(rstd[:, t % 4, :], mv[:, t % 4, 1:2], neghalf[:, 0, :], ALU.pow).then_inc(rstd_ready, 1)
                if t == 3:
                    pool.wait_ge(wghi_ready, 1)
                    sub_hi(wglo[:, :, :], wgr[:, :, :], wghi[:, :, :]).then_inc(wglo_ready, 1)
            for t in range(NT):
                pool.wait_ge(h1hi_ready, t + 1)
                sub_hi(h1lo[:, :, chunk(t)], hm[:, t % 2, :, :], h1hi[:, :, chunk(t)]).then_inc(h1lo_ready, 1)

            tt = nc.gpsimd.tensor_tensor
            pool.wait_ge(inv_in, 16)
            pool.wait_ge(pe_ada, N_ADA1)
            for g, win in enumerate(WINDOWS):
                steps = win.bit_length() - 1
                xg = qk[:, H + g, :]
                pool.wait_ge(tile_out, g + 1)
                if g:
                    pool.wait_ge(pool_y, g)
                link(nc.gpsimd.memset(poolA[:, :], 0.0))
                link(nc.gpsimd.tensor_copy(poolA[:, 8 * GRID_W:24 * GRID_W], xg[:, 0:LAT]))
                a, b = poolA, poolB
                for lv in range(1, steps + 1):
                    ext = win // 2 - (1 << (lv - 1))
                    lo_r, n_r = 8 - ext, GRID_H + 2 * ext
                    back, ahead = (1, 0) if lv == 1 else (1 << (lv - 2), 1 << (lv - 2))
                    link(tt(b[:, lo_r * GRID_W:(lo_r + n_r) * GRID_W],
                            a[:, (lo_r - back) * GRID_W:(lo_r - back + n_r) * GRID_W],
                            a[:, (lo_r + ahead) * GRID_W:(lo_r + ahead + n_r) * GRID_W], ALU.add))
                    a, b = b, a
                nlat = GRID_H * PADW
                link(nc.gpsimd.memset(b[:, 0:nlat + PADC], 0.0))

                def padded(buf):
                    return (buf[:, 0:nlat].rearrange("p (r w) -> p r w", w=PADW), buf[:, nlat:nlat + PADC])
                link(nc.gpsimd.tensor_copy(padded(b)[0][:, :, 8:8 + GRID_W],
                                           a[:, 8 * GRID_W:24 * GRID_W].rearrange("p (r w) -> p r w", w=GRID_W)))
                link(nc.gpsimd.tensor_copy(padded(b)[1][:, 8:8 + CTX], xg[:, LAT:T]))
                a, b = b, a
                for lv in range(1, steps + 1):
                    ext = win // 2 - (1 << (lv - 1))
                    back, ahead = (1, 0) if lv == 1 else (1 << (lv - 2), 1 << (lv - 2))
                    at = 8 - ext
                    (al, ac), (bl, bctx) = padded(a), padded(b)
                    for dst, src, n_c in ((bl, al, GRID_W + 2 * ext), (bctx, ac, CTX + 2 * ext)):
                        link(tt(dst[..., at:at + n_c], src[..., at - back:at - back + n_c],
                                src[..., at + ahead:at + ahead + n_c], ALU.add))
                    a, b = b, a
                al, ac = padded(a)
                bl, bctx = padded(b)
                res, xl = al[:, :, 8:8 + GRID_W], xg[:, 0:LAT].rearrange("p (r w) -> p r w", w=GRID_W)
                mid = bl[:, :, 8:8 + GRID_W]
                link(tt(mid, res, bc(invt[:, g, 0:GRID_H].unsqueeze(2), [P, GRID_H, GRID_W]), ALU.mult))
                link(tt(res, mid, bc(invt[:, g, GRID_H:GRID_H + GRID_W].unsqueeze(1), [P, GRID_H, GRID_W]), ALU.mult))
                link(tt(bctx[:, 8:8 + CTX], ac[:, 8:8 + CTX], invt[:, g, GRID_H + GRID_W:], ALU.mult))
                link(tt(xl, res, xl, ALU.subtract))
                tt(xg[:, LAT:T], bctx[:, 8:8 + CTX], xg[:, LAT:T], ALU.subtract).then_inc(pool_y, 1)

            def po_lo(j):
                pool.wait_ge(pohi_ready, j + 1)
                if j >= 1:
                    pool.wait_ge(polo_out, 16 * j)
                sub_hi(polo[:, :], po[:, :], pohi[:, :]).then_inc(polo_ready, 1)

            def lo(n):
                pool.wait_ge(whi_ready, n + 1)
                sub_hi(wlo[:, n % 2, :], raw[:, n % RAWN, :], whi[:, n % 2, :]).then_inc(wlo_pool, 1)

            def select(s, d):
                pool.wait_ge(d_exp[d], s + 1)
                D = Dm[:, s % 2, d, :, :]
                sgn = 1 if d == 0 else -1
                nc.gpsimd.affine_select(out=D, in_=D, compare_op=ALU.is_ge, fill=0.0, base=0,
                                        pattern=[[0, H], [sgn, P]], channel_multiplier=-sgn).then_inc(d_sel[d], 1)
                if s < LT:
                    ck = scan_chunks(s)[d]
                    pool.wait_ge(qa_in[d], 16 * (s + 1))
                    if s == 0 and d == 0:
                        pool.wait_ge(silu_done, 2 * H)
                    tt(Qa[:, d, :, :], Qa[:, d, :, :], qk[:, 0:H, chunk(ck)], ALU.mult).then_inc(qa_ready[d], 1)

            for n in range(23, 2 * NPROJ):
                po_lo(n - 23)
                if n + 2 >= U_LO:
                    lo(n + 2)
            po_lo(9)
            po_lo(10)
            po_lo(11)
            fin = 0
            select(0, 0)
            select(0, 1)
            for s in range(NSTEP):
                n = U_C + s + 2
                if n < U_OUT or n == U_OUT + 1:
                    lo(n)
                if s == LT - 1:
                    pool.wait_ge(pohi_out, 16 * 12)
                    pool.wait_ge(polo_out, 16 * 12)
                    pool.wait_ge(pe_unit, U_OUT)
                    pool.dma_start(mixhi[:, 0:H, :], pool_out[0].bitcast(F32R)).then_inc(pool_back, 16)
                    pool.dma_start(mixlo[:, 0:H, :], pool_out[1].bitcast(F32R)).then_inc(pool_back, 16)
                n_fin = len([ck for at, ck in final if at == s - 1])
                for _ in range(n_fin):
                    pool.wait_ge(hvar_ready, fin + 1)
                    tt(rsh[:, fin % 2, :, :], mvh[:, fin % 2, :, 1:2], neghalf[:, :, :], ALU.pow).then_inc(hrstd_ready, 1)
                    fin += 1
                if s + 1 < NSTEP:
                    select(s + 1, 0)
                    select(s + 1, 1)
            pool.wait_ge(hvar_ready, fin + 1)
            tt(rsh[:, fin % 2, :, :], mvh[:, fin % 2, :, 1:2], neghalf[:, :, :], ALU.pow).then_inc(hrstd_ready, 1)

            def mix_lo(g):
                pool.wait_ge(mixhi_ready, g + 1)
                sub_hi(mixlo[:, H:2 * H, grp(g)], qk[:, 0:H, grp(g)], mixhi[:, H:2 * H, grp(g)]).then_inc(mixlo_ready, 1)

            def rstd_ln(j):
                pool.wait_ge(lvar, j + 1)
                tt(rstd[:, j % 4, :], mv[:, j % 4, 1:2], neghalf[:, 0, :], ALU.pow).then_inc(lrstd, 1)

            def h2_lo(t):
                pool.wait_ge(h2hi_ready, t + 1)
                pool.wait_ge(h2lo_ready, t)
                sub_hi(h2lo[:, :, chunk(t)], hm2[:, :, :], h2hi[:, :, chunk(t)]).then_inc(h2lo_ready, 1)

            def gain_mult(buf, t, rows, count):
                pool.wait_ge(lnorm, count)
                tt(buf[:, t % 4, :], buf[:, t % 4, :], rows[:, 0, :], ALU.mult).then_inc(g_mult, 1)

            def gain_add(buf, t, rows, count, done):
                pool.wait_ge(g_mult, count)
                tt(buf[:, t % 4, :], buf[:, t % 4, :], rows[:, 1, :], ALU.add).then_inc(done, 1)

            for g in range(NG):
                if g == 1:
                    pool.wait_ge(ln_in, 32)
                j0, t0 = 2 * GT * (g - 1), GT * (g - 1)
                for r in range(2 * KT):
                    n = U_OUT + g * 2 * KT + r + 2
                    if n % 2 or n >= U_UP:
                        lo(n)
                    if g == 0 and r in (2, 5, 8):
                        mix_lo((r - 2) // 3)
                    if g >= 1:
                        if r in (3, 4, 5):
                            rstd_ln(j0 + r - 3)
                        if r in (10, 12, 13):
                            rstd_ln(j0 + GT + (10, 12, 13).index(r))
                        if r in (6, 8, 10):
                            t = t0 + (r - 6) // 2
                            gain_mult(yt, t, lnrows, t + 1)
                        if r in (7, 9, 11):
                            t = t0 + (r - 7) // 2
                            gain_add(yt, t, lnrows, t + 1, x1_ready)
            j0, a, b = 2 * GT * (NG - 1), NT - 3, NT - 2
            rstd_ln(j0)
            gain_mult(yt, a, lnrows, a + 1)
            rstd_ln(j0 + 1)
            gain_add(yt, a, lnrows, a + 1, x1_ready)
            rstd_ln(j0 + 2)
            rstd_ln(j0 + 3)
            rstd_ln(j0 + 4)
            h2_lo(a)
            rstd_ln(j0 + 5)
            h2_lo(b)

            def up_tile(i):
                for q in range(4):
                    m = q + 2
                    pool.wait_ge(whi_ready, 4 * i + (U_UP + m + 1))
                    sub_hi(wlo[:, m % 2, :], raw[:, m % 4, :], whi[:, m % 2, :]).then_inc(wlo_pool, 1)

            with pool.Fori(0, FT - 1) as i:
                up_tile(i)
            lo(U_DOWN - 2)
            lo(U_DOWN - 1)
            lo(U_DOWN + 1)

            def down_pair(g, pair, last_pair=False):
                base = U_DOWN + g * 2 * FT
                for q in (1, 3):
                    if not (last_pair and g == NG - 1 and q >= 2):
                        m = q + 2
                        pool.wait_ge(whi_ready, 4 * pair + (base + m + 1))
                        sub_hi(wlo[:, m % 2, :], raw[:, m % 4, :], whi[:, m % 2, :]).then_inc(wlo_pool, 1)
                    if not (last_pair and g == NG - 1):
                        pool.wait_ge(ushi_ready, 2 * pair + (g * FT + 2 + q // 2 + 1))
                        src = u[:, q // 2, grp(g + 1)] if last_pair else u[:, bass.ds(2 * pair + (2 + q // 2), 1), grp(g)]
                        sub_hi(uslo[:, q // 2, :], src, ushi[:, q // 2, :]).then_inc(uslo_ready, 1)

            for b in range(2):
                pool.wait_ge(ushi_ready, b + 1)
                sub_hi(uslo[:, b, :], u[:, b, grp(0)], ushi[:, b, :]).then_inc(uslo_ready, 1)
            for g in range(NG):
                down_pair(g, 0)
                down_pair(g, 1)
                if g >= 1:
                    for i in range(GT):
                        rstd_ln(2 * NT + (g - 1) * GT + i)
                down_pair(g, 2)
                if g == 0:
                    pool.wait_ge(ln2_in, 32)
                    with pool.Fori(3, 9) as pair:
                        down_pair(g, pair)
                else:
                    for i in range(GT):
                        t = (g - 1) * GT + i
                        down_pair(g, 3 + 2 * i)
                        gain_mult(zt, t, lnrows2, NT + t + 1)
                        down_pair(g, 4 + 2 * i)
                        gain_add(zt, t, lnrows2, N_GM + t + 1, z_ready)
                with pool.Fori(9, FT // 2 - 1) as pair:
                    down_pair(g, pair)
                down_pair(g, FT // 2 - 1, last_pair=True)
            j0, a = 2 * NT + (NG - 1) * GT, NT - 3
            rstd_ln(j0)
            gain_mult(zt, a, lnrows2, NT + a + 1)
            rstd_ln(j0 + 1)
            gain_add(zt, a, lnrows2, N_GM + a + 1, z_ready)
            rstd_ln(j0 + 2)

        @block.vector
        def _(dve):
            link = chain(dve, dve_chain)
            v = nc.vector
            tt, tsc, stt = v.tensor_tensor, v.tensor_scalar, v.scalar_tensor_tensor
            v.memset(one11[:, :], 1.0)
            v.memset(pick[:, :, :], 0.0).then_inc(ones_ready, 1)
            dve.wait_ge(ones_ready, 1)
            for w in both:
                v.memset(pick[:, w, w:w + 1], 1.0)
            v.memset(neghalf[:, :, :], -0.5).then_inc(consts_ready, 1)

            def norm_stats(buf, slot, count, ready, load, load_count):
                dve.wait_ge(load, load_count)
                for b in range(2):
                    ins = v.bn_stats(stats[:, slot, 6 * b:6 * b + 6], buf[:, b * 512:(b + 1) * 512])
                link(ins)
                link(v.bn_aggr(mv[:, slot, :], stats[:, slot, :]))
                tsc(mv[:, slot, 1:2], mv[:, slot, 1:2], EPS, None, ALU.add).then_inc(ready, 1)

            def normalise(out, buf, slot, ready, count):
                dve.wait_ge(ready, count)
                return tsc(out, buf, mv[:, slot, 0:1], rstd[:, slot, :], ALU.subtract, ALU.mult)

            def x_norm(t):
                normalise(xt[:, t, :], xt[:, t, :], t % 4, rstd_ready, t + 1).then_inc(xn_ready, 1)

            for t in range(NT):
                norm_stats(xt[:, t, :], t % 4, t, var_ready, x_in[t % 3], 16 * (t // 3 + 1))
                if t >= 1:
                    x_norm(t - 1)
            x_norm(NT - 1)

            def ada_evac(b0, b1):
                link(tt(adaT[:, b0:b1, :], ps[:, 6, 2 * b0:2 * b1].rearrange("p (b w) -> p b w", w=2),
                        bc(colv[:, V_BADA + b0:V_BADA + b1].unsqueeze(2), [P, b1 - b0, 2]), ALU.add))

            dve.wait_ge(pe_adaT, 1)
            dve.wait_ge(cols_ready, 2)
            ada_evac(0, A_G1)
            tsc(ada1p[:, 0, :, :], adaT[:, A_SC1:A_SC1 + KT, :], 1.0, None, ALU.add).then_inc(ada_a, 1)
            dve.wait_ge(ada_a, 1)

            def modulate(out, bank, t, which, shift):
                w = who(t)
                for k in range(KT // 2, KT):
                    last = tsc(out[:, k, :], ps[:, bank, (k % 4) * P:(k % 4 + 1) * P], ada1p[:, which, k, w:w + 1],
                               adaT[:, shift + k, w:w + 1], ALU.mult, ALU.add)
                return last

            def lo(n):
                dve.wait_ge(whi_ready, n + 1)
                tt(wlo[:, n % 2, :], raw[:, n % RAWN, :], whi[:, n % 2, :].bitcast(F32), ALU.subtract).then_inc(wlo_dve, 1)

            def graw_evac(g):
                dve.wait_ge(pe_gate, g + 1)
                v.tensor_copy(graw[:, grp(g)], ps[0:NGATE, 7, 0:GN]).then_inc(graw_ready, 1)

            for t in range(NT):
                dve.wait_ge(pe_xT, t + 1)
                if t >= 2:
                    dve.wait_ge(h1lo_ready, t - 1)
                modulate(hm[:, t % 2, :, :], 2 * (t % 3) + 1, t, 0, A_SH1).then_inc(hm_dve, 1)
                if t == 5:
                    lo(0)
                    lo(1)
                if t >= 5 and t != 6 and t != 7:
                    graw_evac(0 if t == 5 else 1)
            graw_evac(2)

            v.memset(onesr[:, :], 1.0)
            v.memset(gi[:, :], 0.0)
            link(v.memset(gf[:, :], 0.0))
            dve.wait_ge(bg_in, 16)
            dve.wait_ge(pe_gate, NG + 1)
            gp = ps[:, 7, 0:NT * NGATE].rearrange("p (c g) -> p g c", g=NGATE)
            for typ in range(4):
                dst = (gi, gf)[typ % 2]
                d = typ // 2
                last = tt(dst[:, DIR * d:DIR * d + H * NT].rearrange("p (h c) -> p h c", c=NT),
                          gp[:, typ * H:(typ + 1) * H, :],
                          bc(bgate[:, typ * H:(typ + 1) * H].unsqueeze(2), [P, H, NT]), ALU.add)
            last.then_inc(gates_ready, 1)

            def gate_chain1():
                dve.wait_ge(pe_gT, 1)
                v.tensor_copy(li[:, :], ps[:, 7, 0:P])
                link(v.tensor_copy(fr[:, :], ps[:, 7, P:2 * P]))
                stt(lf[:, :], fr[:, :], -1.0, fr[:, :], ALU.mult, ALU.max).then_inc(f_abs, 1)

            def gate_chain2():
                dve.wait_ge(ln_ready, 1)
                link(stt(lf[:, :], fr[:, :], 0.0, Wr[:, :], ALU.min, ALU.subtract))
                fw, bw = slice(0, DIR), slice(DIR, P)
                v.tensor_tensor_scan(Bc[fw, :], onesr[fw, :], lf[fw, :], 0.0, ALU.mult, ALU.add)
                link(v.tensor_tensor_scan(Bc[bw, ::-1], onesr[bw, :], lf[bw, ::-1], 0.0, ALU.mult, ALU.add))
                link(tt(Ac[:, :], li[:, :], Bc[:, :], ALU.subtract))
                v.tensor_tensor_scan(CM[fw, :], Ac[fw, :], Ac[fw, :], -3.0e38, ALU.max, ALU.max)
                v.tensor_copy(gcol[fw, 0:1], Bc[fw, P - 1:P])
                link(v.tensor_tensor_scan(CM[bw, ::-1], Ac[bw, ::-1], Ac[bw, ::-1], -3.0e38, ALU.max, ALU.max))
                link(v.tensor_copy(gcol[bw, 0:1], Bc[bw, 0:1]))
                tt(gcol[fw, 1:2], gcol[fw, 0:1], CM[fw, P - 1:P], ALU.add)
                link(tt(gcol[bw, 1:2], gcol[bw, 0:1], CM[bw, 0:1], ALU.add))
                v.memset(mrow[:, :], 0.0).then_inc(rows_ready, 1)

            def gate_chain3():
                dve.wait_ge(pe_grow, 1)
                dve.wait_ge(m0_in, 16)
                dve.wait_ge(rows_ready, 1)
                link(v.tensor_copy(grow[:, :, :], ps[0:1, 7, 0:2 * P].rearrange("p (a b) -> p a b", b=P)))
                for d in both:
                    first = 0 if d == 0 else LT - 1
                    link(v.tensor_copy(mrow[:, rows_of(d, first)], m0row[:, d * H:(d + 1) * H]))
                for d in both:
                    for h in range(H):
                        r = row0(d, 0) + NT * h
                        if d == 0:
                            src, dst = slice(r, r + LT - 1), slice(r + 1, r + LT)
                        else:
                            src, dst = slice(r + LT - 1, r, -1), (slice(r + LT - 2, r - 1, -1) if r else slice(LT - 2, None, -1))
                        last = v.tensor_tensor_scan(mrow[:, dst], grow[:, 0, src], grow[:, 1, src],
                                                    m0row[:, d * H + h:d * H + h + 1], ALU.add, ALU.max)
                last.then_inc(mrow_ready, 1)

            def gate_chain4():
                dve.wait_ge(pe_mcol, 1)
                link(v.tensor_copy(gcol[:, 2:3], ps[:, 7, 0:1]))
                tsc(nM[:, :], CM[:, :], gcol[:, 2:3], -1.0, ALU.max, ALU.mult)
                link(tt(gcol[:, 6:7], gcol[:, 0:1], gcol[:, 2:3], ALU.add))
                link(tt(gcol[:, 3:4], gcol[:, 6:7], gcol[:, 1:2], ALU.max))
                tt(gcol[:, 4:5], gcol[:, 6:7], gcol[:, 3:4], ALU.subtract)
                link(tt(gcol[:, 5:6], gcol[:, 0:1], gcol[:, 3:4], ALU.subtract))
                tt(enm[:, :], nM[:, :], Bc[:, :], ALU.subtract).then_inc(exps_in, 1)

            def gate_chain5():
                dve.wait_ge(pe_tok, 1)
                v.tensor_copy(tok[:, 0, :], ps[:, 7, 0:P])
                tsc(tok[:, 1, :], ps[:, 7, P:2 * P], QK_SCALE, None, ALU.mult)
                v.tensor_copy(tok[:, 2, :], ps[:, 7, 2 * P:3 * P])
                v.tensor_copy(decb[:, :], ps[:, 7, 3 * P:4 * P]).then_inc(tok_ready, 1)
                dve.wait_ge(pe_ada, N_ADA1)
                v.memset(v1[:, :, :, P:P + 1], 1.0).then_inc(v_ready, 1)

            def v_evac(h, part):
                j = 3 * h + part
                dve.wait_ge(pe_v, j + 1)
                c0, c1 = 4 * part, min(4 * part + 4, NT)
                v.tensor_copy(v1[:, c0:c1, h, 0:P], ps[:, 7, 0:(c1 - c0) * P].rearrange("p (c n) -> p c n", n=P)
                              ).then_inc(v_ready, 1)

            def conv(j):
                tile = 2 * H + j
                dve.wait_ge(tile_out, tile + 1)
                if j < H:
                    dve.wait_ge(pe_v, 3 * (j + 1))
                else:
                    dve.wait_ge(pe_pool, 3 * (j - H + 1))
                src, dst = work[:, tile % 2, :], qk[:, j, :]
                w = [colv[:, V_CONV + KT * a + j:V_CONV + KT * a + j + 1] for a in range(3)]
                if j >= N_ACT_TAP:
                    link(tsc(dst, src, w[1], None, ALU.mult))
                for a in (0, 2):
                    for t0, t1 in ((0, LAT), (LAT, T)):
                        o, i_ = (slice(t0 + 1, t1), slice(t0, t1 - 1)) if a == 0 else (slice(t0, t1 - 1), slice(t0 + 1, t1))
                        last = stt(dst[:, o], src[:, i_], w[a], dst[:, o], ALU.mult, ALU.add)
                    if a == 0:
                        link(last)
                last.then_inc(conv_done, 1)

            def arow_evac(j):
                dve.wait_ge(pe_ada, j + 1)
                v.tensor_copy(arow[:, j % 2, :], ps[0:2, 6, ADA_AT:ADA_AT + AC]).then_inc(arow_ready, 1)

            def ada_half(n):
                dve.wait_ge(ada_in[n % 2], 16 * (n // 2 + 1))
                if n >= 2 and n % 2 == 0:
                    dve.wait_ge(pe_ada, N_ADA1 + n // 2)
                for k in range(KT // 2):
                    kk = (n % 2) * KT // 2 + k
                    for w, v0 in enumerate((V_C, V_CC)):
                        s_col = colv[:, v0 + kk:v0 + kk + 1]
                        if kk == 0:
                            last = tsc(aacc[:, w, :], adaw[:, n % 2, k, :], s_col, None, ALU.mult)
                        else:
                            last = stt(aacc[:, w, :], adaw[:, n % 2, k, :], s_col, aacc[:, w, :], ALU.mult, ALU.add)
                    if k < KT // 2 - 1:
                        link(last)
                last.then_inc(ada_used, 1)
                dve.wait_ge(ada_used, n + 1)

            for n in range(2 * NPROJ):
                if n >= 3 and n % 2:
                    arow_evac(N_ADA1 + (n - 3) // 2)
                job = JOBS.get(n - 1, ("",))
                if job[0] == "v":
                    v_evac(job[1], job[2])
                if n == 9:
                    gate_chain5()
                if n == 5:
                    gate_chain3()
                if n == 7:
                    gate_chain4()
                if n + 2 < U_LO:
                    lo(n + 2)
                if n == 2:
                    gate_chain1()
                if n == 3:
                    gate_chain2()
                ada_half(n)
                if n % 2 == 0 and n // 2 > 2 * H:
                    conv(n // 2 - 1 - 2 * H)
            arow_evac(N_ADA - 1)
            conv(2 * H - 1)
            dve.wait_ge(pe_adaT, 2)
            ada_evac(A_G1, 6 * KT)
            tsc(ada1p[:, 1, :, :], adaT[:, A_SC2:A_SC2 + KT, :], 1.0, None, ALU.add).then_inc(ada_b, 1)

            dve.wait_ge(tok_ready, 1)

            def head_cols(table, d, ck, shape):
                return bc(table[:, rows_of(d, ck)].unsqueeze(2), shape)

            def d_add(s, d):
                ck = scan_chunks(s)[d]
                D = Dm[:, s % 2, d, :, :]
                dve.wait_ge(dm_in[s % 2][d], 16 * (s // 2 + 1))
                tt(D, D, head_cols(tok[:, 0, :], d, ck, [P, H, P]), ALU.add).then_inc(d_added[d], 1)

            def p_make(s, d):
                dve.wait_ge(pe_s[d], s + 1)
                dve.wait_ge(d_sel[d], s + 1)
                D = Dm[:, s % 2, d, :, :].rearrange("p h n -> p (h n)")
                stt(D, ps[:, 3 + d, :], QK_SCALE, D, ALU.mult, ALU.mult).then_inc(p_ready[d], 1)

            def kw_make(s, d):
                ck = scan_chunks(s)[d]
                dve.wait_ge(pe_kt[d], s + 1)
                if s >= 1:
                    dve.wait_ge(pe_u[d], 2 * s if s < LT else 2 * s - 2)
                tt(kw[:, d, :, :], ps[:, 5, :].rearrange("p (h n) -> p h n", h=H),
                   head_cols(tok[:, 1, :], d, ck, [P, H, P]), ALU.mult).then_inc(kw_ready[d], 1)

            seen = set()

            def num_evac(s, d):
                ck = scan_chunks(s)[d]
                for pair in range(2):
                    dve.wait_ge(pe_num[d], 2 * s + pair + 1)
                    acc2 = ps[:, 6 + pair, 0:2 * (P + 1)].rearrange("p (h n) -> p h n", h=2)
                    r = rows_of(d, ck)
                    em = tok[:, 2, r][:, 2 * pair:2 * pair + 2].unsqueeze(2)
                    link(stt(rden[:, :, :], acc2[:, :, P:P + 1], -1.0, em, ALU.mult, ALU.max))
                    link(tt(rden[:, :, :], rden[:, :, :], acc2[:, :, P:P + 1], ALU.max))
                    link(v.reciprocal(rden[:, :, :], rden[:, :, :]))
                    out = hacc[:, ck, 2 * pair:2 * pair + 2, :]
                    rb = bc(rden[:, :, :], [P, 2, P])
                    if (ck, pair) not in seen:
                        seen.add((ck, pair))
                        ins = tt(out, acc2[:, :, 0:P], rb, ALU.mult)
                        ins.then_inc(num_used[d], 1)
                        dve.wait_ge(num_used[d], 2 * s + pair + 1)
                    else:
                        ins = tt(tmph[:, :, :], acc2[:, :, 0:P], rb, ALU.mult)
                        ins.then_inc(num_used[d], 1)
                        dve.wait_ge(num_used[d], 2 * s + pair + 1)
                        link(tt(out, out, tmph[:, :, :], ALU.add))

            def u_add(s, d):
                ck = scan_chunks(s)[d]
                for pair in range(2):
                    dve.wait_ge(pe_u[d], (2 * s if s < LT else 2 * s - 2) + pair + 1)
                    for hh in range(2):
                        h = 2 * pair + hh
                        add = ps[:, 6 + pair, hh * (P + 1):(hh + 1) * (P + 1)]
                        r = row0(d, ck) + NT * h
                        if s < LT:
                            last = stt(Cs[:, d, h, :], Cs[:, d, h, :], decb[:, r:r + 1], add, ALU.mult, ALU.add)
                        else:
                            last = v.tensor_copy(Cs[:, d, h, :], add)
                    last.then_inc(u_used[d], 1)

            fin = [0, 0]

            def h_stats():
                ck = final[fin[0]][1]
                b = fin[0] % 2
                for h in range(H):
                    last = v.bn_stats(sth[:, b, h, :], hacc[:, ck, h, :])
                link(last)
                for h in range(H):
                    last = v.bn_aggr(mvh[:, b, h, :], sth[:, b, h, :])
                link(last)
                tsc(mvh[:, b, :, 1:2], mvh[:, b, :, 1:2], EPS, None, ALU.add).then_inc(hvar_ready, 1)
                fin[0] += 1

            def h_norm():
                ck = final[fin[1]][1]
                b = fin[1] % 2
                dve.wait_ge(hrstd_ready, fin[1] + 1)
                hc = hacc[:, ck, :, :]
                link(tt(hc, hc, bc(mvh[:, b, :, 0:1], [P, H, P]), ALU.subtract))
                tt(hc, hc, bc(rsh[:, b, :, :], [P, H, P]), ALU.mult).then_inc(hn_ready, 1)
                fin[1] += 1

            d_add(0, 0)
            d_add(0, 1)
            dve.wait_ge(cs_in, 64)
            for s in range(NSTEP):
                if s == LT:
                    lo(U_OUT)
                p_make(s, 0)
                p_make(s, 1)
                kw_make(s, 0)
                if 1 <= s < LT:
                    u_add(s - 1, 1)
                if s + 1 < NSTEP:
                    d_add(s + 1, 0)
                kw_make(s, 1)
                num_evac(s, 0)
                if s + 1 < NSTEP:
                    d_add(s + 1, 1)
                for _ in [ck for at, ck in final if at == s - 1]:
                    h_norm()
                num_evac(s, 1)
                if s < LT - 1 or s == LT:
                    u_add(s, 0)
                for _ in [ck for at, ck in final if at == s]:
                    h_stats()
            u_add(LT, 1)
            h_norm()

            def ml(g):
                dve.wait_ge(sig_ready, 1)
                dve.wait_ge(hT_used, LT if g < NG - 1 else NT)
                for h in range(H):
                    last = stt(qk[:, h, grp(g)], qk[:, h, grp(g)], colv[:, V_HN + h:V_HN + h + 1], work[:, h, grp(g)],
                               ALU.mult, ALU.mult)
                last.then_inc(ml_ready, 1)

            nst = [0]

            def residual(t, buf, tmp, rows, out_sem, out_count, used, before):
                g, i = t // GT, t % GT
                dve.wait_ge(y_in[t % 4], 16 * (t // 4 + 1 + before * times(t % 4)))
                for half in range(2):
                    dve.wait_ge(out_sem, out_count(g, i, half))
                    cols = slice(half * 512, (half + 1) * 512)
                    tt(tmp[:, cols], ps[:, (down_bank if before else out_bank)(g, 2 * i + half), :], rows[:, who(t), cols], ALU.mult).then_inc(used, 1)
                dve.wait_ge(used, 2 * (t + 1))
                link(stt(buf[:, t % 4, :], buf[:, t % 4, :], ALPHA, tmp[:, :], ALU.mult, ALU.add))

            def ln_stats(buf):
                slot = nst[0] % 4
                for b in range(2):
                    ins = v.bn_stats(stats[:, slot, 6 * b:6 * b + 6], buf[:, b * 512:(b + 1) * 512])
                link(ins)
                link(v.bn_aggr(mv[:, slot, :], stats[:, slot, :]))
                tsc(mv[:, slot, 1:2], mv[:, slot, 1:2], EPS, None, ALU.add).then_inc(lvar, 1)
                nst[0] += 1

            def ln_norm(out, buf, j):
                return normalise(out, buf, j % 4, lrstd, j + 1)

            dve.wait_ge(ada_b, 1)
            def res1(t):
                if t >= 1:
                    dve.wait_ge(pe_yT, t // GT * GT)
                residual(t, yt, tb, grows, pe_unit, lambda g, i, half: U_OUT + (g + 1) * KT * 2, out_used, 0)

            def norm1(t):
                ln_norm(yt[:, t % 4, :], yt[:, t % 4, :], 2 * GT * (t // GT) + t % GT).then_inc(lnorm, 1)

            def stats2(t):
                dve.wait_ge(x1_ready, t + 1)
                ln_stats(yt[:, t % 4, :])

            def norm2(t):
                if t >= 1:
                    dve.wait_ge(pe_yT, t)
                ln_norm(tb[:, :], yt[:, t % 4, :], 2 * GT * (t // GT) + GT + t % GT).then_inc(tb_ready, 1)

            def h2_lo(t):
                dve.wait_ge(h2hi_ready, t + 1)
                tt(h2lo[:, :, chunk(t)], hm2[:, :, :], h2hi[:, :, chunk(t)].bitcast(F32), ALU.subtract).then_inc(h2lo_ready, 1)

            def gain_both(buf, t, rows, count, done):
                dve.wait_ge(lnorm, count)
                link(tt(buf[:, t % 4, :], buf[:, t % 4, :], rows[:, 0, :], ALU.mult))
                tt(buf[:, t % 4, :], buf[:, t % 4, :], rows[:, 1, :], ALU.add).then_inc(done, 1)

            for g in range(NG):
                if g == 1:
                    dve.wait_ge(grows_in, 32)
                a, b, c_ = (GT * (g - 1) + i for i in range(GT))
                steps = {0: (res1, c_), 2: (ln_stats, yt[:, a % 4, :]), 3: (ln_stats, yt[:, b % 4, :]),
                         4: (ln_stats, yt[:, c_ % 4, :]), 9: (stats2, a), 10: (norm2, a), 11: (stats2, b),
                         12: (norm2, b), 14: (norm2, c_), 15: (h2_lo, b)}
                if g >= 1:
                    res1(a)
                    res1(b)
                for r in range(2 * KT):
                    n = U_OUT + g * 2 * KT + r + 2
                    if n % 2 == 0 and n < U_UP:
                        lo(n)
                    if g == 0 and r in (1, 3, 5):
                        ml(r // 2)
                    if g >= 1:
                        if r == 1 and g >= 2:
                            h2_lo(a - 1)
                        if r in steps:
                            step, arg = steps[r]
                            step(arg)
                        if r == 5:
                            norm1(a)
                            norm1(b)
                        if r == 6:
                            norm1(c_)
                        if r == 13:
                            stats2(c_)
                            h2_lo(a)
            a, b, c_ = range(NT - GT, NT)
            dve.wait_ge(ln_in, 32)
            j0 = 2 * GT * (NG - 1)

            def norm_first(t, n):
                ln_norm(yt[:, t % 4, :], yt[:, t % 4, :], j0 + n).then_inc(lnorm, 1)

            def norm_second(t, n):
                dve.wait_ge(pe_yT, t)
                ln_norm(tb[:, :], yt[:, t % 4, :], j0 + n).then_inc(tb_ready, 1)

            res1(a)
            h2_lo(a - 1)
            ln_stats(yt[:, a % 4, :])
            res1(b)
            norm_first(a, 0)
            ln_stats(yt[:, b % 4, :])
            res1(c_)
            norm_first(b, 1)
            stats2(a)
            ln_stats(yt[:, c_ % 4, :])
            norm_second(a, 2)
            gain_both(yt, b, lnrows, b + 1, x1_ready)
            stats2(b)
            norm_first(c_, 3)
            norm_second(b, 4)
            gain_both(yt, c_, lnrows, c_ + 1, x1_ready)
            stats2(c_)
            norm_second(c_, 5)
            dve.wait_ge(h2lo_ready, c_)
            h2_lo(c_)

            lat3 = [x[:, 0:LAT].rearrange("p (r w) -> p r w", w=GRID_W) for x in (gs, acc)]

            others = [(dy, dx) for dx in (-1, 0, 1) for dy in (-1, 0, 1) if (dy, dx) != (0, 0)]
            n_conv = len(others) + 3

            def shifted(n, d):
                return slice(max(0, -d), n - max(0, d)), slice(max(0, d), n - max(0, -d))

            def up_tile(i, last_tile=False):
                def step(ins, m):
                    ins.then_inc(conv_step, 1)
                    dve.wait_ge(conv_step, n_conv * i + m)

                dve.wait_ge(g_out, i + 1)
                v.tensor_copy(taps[:, 0:NTAP], dwc[:, :].rearrange("p (t f) -> p t f", f=FT)[:, :, bass.ds(i, 1)])
                step(v.tensor_copy(taps[:, NTAP:NTAP + 1], colv[:, bass.ds(i + V_BDW, 1)]), 1)
                step(tsc(acc[:, :], gs[:, :], taps[:, 4:5], None, ALU.mult), 2)
                for m, (dy, dx) in enumerate(others):
                    tap = 3 * (dy + 1) + dx + 1
                    (ro, ri), (co, ci) = shifted(GRID_H, dy), shifted(GRID_W, dx)
                    step(stt(lat3[1][:, ro, co], lat3[0][:, ri, ci], taps[:, tap:tap + 1], lat3[1][:, ro, co],
                             ALU.mult, ALU.add), 3 + m)
                for dx in (-1, 1):
                    co, ci = shifted(CTX, dx)
                    ins = stt(acc[:, LAT:T][:, co], gs[:, LAT:T][:, ci], taps[:, 4 + dx:5 + dx], acc[:, LAT:T][:, co],
                              ALU.mult, ALU.add)
                    if dx < 0:
                        step(ins, n_conv)
                    else:
                        ins.then_inc(conv_ready, 1)
                if last_tile:
                    lo(U_DOWN)
                dve.wait_ge(gelu_ready, i + 1)
                dve.wait_ge(pe_unit, 4 * i + (U_UP + 4))
                tt(u[:, bass.ds(i, 1), :].rearrange("p a (g n) -> p (a g) n", g=NG),
                   acc[:, :].rearrange("p (g n) -> p g n", g=NG), ps[:, 3:6, 0:GN], ALU.mult).then_inc(u_ready, 1)

            up_tile(0)
            for b in range(4):
                dve.wait_ge(y_out[b], 16 * times(b))
            with dve.Fori(1, FT - 1) as i:
                up_tile(i)
            up_tile(FT - 1, last_tile=True)

            def res2(t):
                residual(t, zt, zb, grows2, pe_unit, lambda g, i, half: U_DOWN + (g + 1) * 2 * FT - 1 + half, down_used, 1)

            def norm3(t):
                ln_norm(zt[:, t % 4, :], zt[:, t % 4, :], 2 * NT + t).then_inc(lnorm, 1)

            def down_pair(g, pair, last_pair=False):
                base = U_DOWN + g * 2 * FT
                for m in (2, 4):
                    if not (last_pair and g == NG - 1 and m >= 4):
                        dve.wait_ge(whi_ready, 4 * pair + (base + m + 1))
                        tt(wlo[:, m % 2, :], raw[:, m % 4, :], whi[:, m % 2, :].bitcast(F32), ALU.subtract).then_inc(wlo_dve, 1)

            for g in range(NG):
                tiles = range((g - 1) * GT, g * GT)
                if g == 1:
                    dve.wait_ge(ln2_in, 32)
                    dve.wait_ge(grows_in, 64)
                if g >= 1:
                    res2(tiles[0])
                    res2(tiles[1])
                down_pair(g, 0)
                if g >= 1:
                    res2(tiles[2])
                down_pair(g, 1)
                if g >= 1:
                    for t in tiles:
                        ln_stats(zt[:, t % 4, :])
                down_pair(g, 2)
                if g >= 1:
                    for t in tiles:
                        norm3(t)
                with dve.Fori(3, FT // 2 - 1) as pair:
                    down_pair(g, pair)
                down_pair(g, FT // 2 - 1, last_pair=True)
            a, b, c_ = range(NT - GT, NT)
            res2(a)
            ln_stats(zt[:, a % 4, :])
            res2(b)
            norm3(a)
            ln_stats(zt[:, b % 4, :])
            res2(c_)
            norm3(b)
            ln_stats(zt[:, c_ % 4, :])
            dve.wait_ge(z_ready, b)
            gain_both(zt, b, lnrows2, NT + b + 1, z_ready)
            norm3(c_)
            gain_both(zt, c_, lnrows2, NT + c_ + 1, z_ready)


_INS = ["x_prompt", "x_sample", "c", "state_C", "state_n", "state_m", "c_ctx", "w_ada", "b_ada", "w_in", "b_gates",
        "w_qk_conv", "hn_g", "w_pool", "pool_scale", "w_out", "ln1_g", "ln1_b", "w_up", "w_dw", "b_dw", "w_down",
        "ln2_g", "ln2_b"]
_OUTS = [(1, CTX, DM), (1, LAT, DM), (1, 1, 2, H, P, P), (1, 1, 2, H, P), (1, 1, 2, H)]


def inverse_counts():
    def line(length, w):
        t = np.arange(length)
        return 1.0 / (np.minimum(t + w // 2, length) - np.maximum(t - w // 2, 0))
    return np.stack([np.concatenate([line(GRID_H, w), line(GRID_W, w), line(CTX, w)]) for w in WINDOWS]).astype(np.float32)


def kernel(**inputs):
    import concourse.bacc as _bacc
    from concourse.bass_utils import run_bass_kernel_spmd as _run

    nc = _bacc.Bacc("TRN2", target_bir_lowering=False, num_devices=1)
    arrays, args = {}, []
    for name in _INS + ["inv_count"]:
        a = inverse_counts() if name == "inv_count" else np.ascontiguousarray(inputs[name])
        arrays[f"in_{name}"] = a
        args.append(nc.dram_tensor(f"in_{name}", a.shape, F32, kind="ExternalInput").ap())
    for i, shape in enumerate(_OUTS):
        args.append(nc.dram_tensor(f"out_{i}", shape, F32, kind="ExternalOutput").ap())
    args.append(nc.dram_tensor("scan_rows", (2, P, P), F32).ap())
    args.append(nc.dram_tensor("gate_rows", (2, 2 * KT, P), F32).ap())
    args.append(nc.dram_tensor("pool_out", (2, P, H, T), F32).ap())
    args.append(nc.dram_tensor("x1_rows", (NT, P, DM), F32).ap())
    layer(nc, *args)
    r = _run(nc, [arrays], core_ids=[0])
    return tuple(r.results[0][f"out_{i}"] for i in range(len(_OUTS)))
```
